# Optimizing a Trainium2 kernel written in Bass

```python
import math
import jax
import jax.numpy as jnp
from jax import lax
import numpy as np

D_MODEL = 1024
BATCH = 1
SEQ = 128
DEPTH = 2
DEC_BATCH = 1
DEC_SEQ = 512
PAST_LEN = 128

GRID_W = 64
ROPE_BASE = 10000.0
NORM_EPS = 1e-6
NEG_INF = -1e30
QBLOCK = 128
N_BRANCH = 4
BRANCH_W = 256
RET_H = 4
RET_DK = 64
RET_DV = 64
RET_CHUNK = 128
WIN_HQ = 4
WIN_HKV = 2
WIN_HD = 64
WINDOW = 128
WIN_BLOCK = 128
DIFF_H = 4
DIFF_D = 32
DIFF_DV = 2 * DIFF_D
MLA_H = 4
MLA_NOPE = 64
MLA_ROPE = 32
MLA_V = 64
MLA_QRANK = 256
MLA_KVRANK = 128
D_FF = 2816
CONV_W = 3
IN_SPLITS = (RET_H * RET_DK, RET_H * RET_DK, RET_H * RET_DV, RET_H * RET_DV, WIN_HQ * WIN_HD, WIN_HKV * WIN_HD, WIN_HKV * WIN_HD, DIFF_H * 2 * DIFF_D, DIFF_H * 2 * DIFF_D, DIFF_H * DIFF_DV, MLA_QRANK, MLA_KVRANK, MLA_ROPE)
IN_WIDTH = sum(IN_SPLITS)

kernel_name = 'hybrid_diffusion_step'

def rmsnorm(x, gain):
    xf = x.astype(jnp.float32)
    y = xf * lax.rsqrt(jnp.mean(xf * xf, axis=-1, keepdims=True) + NORM_EPS)
    return (y * gain.astype(jnp.float32)).astype(x.dtype)

def head_layernorm(x):
    xf = x.astype(jnp.float32)
    mu = jnp.mean(xf, axis=-1, keepdims=True)
    var = jnp.mean(jnp.square(xf - mu), axis=-1, keepdims=True)
    return (xf - mu) * lax.rsqrt(var + NORM_EPS)

def _rope_axis(x, pos):
    half = x.shape[-1] // 2
    freqs = ROPE_BASE ** (-jnp.arange(half, dtype=jnp.float32) / half)
    ang = pos.astype(jnp.float32)[:, None] * freqs[None, :]
    cos = jnp.cos(ang)[None, :, None, :]
    sin = jnp.sin(ang)[None, :, None, :]
    xf = x.astype(jnp.float32)
    x1, x2 = xf[..., :half], xf[..., half:]
    return jnp.concatenate([x1 * cos - x2 * sin, x2 * cos + x1 * sin], axis=-1).astype(x.dtype)

def rope_2d(x):
    n_tok = x.shape[1]
    rows = n_tok // GRID_W
    row = jnp.repeat(jnp.arange(rows), GRID_W)
    col = jnp.tile(jnp.arange(GRID_W), rows)
    r = x.shape[-1] // 2
    return jnp.concatenate([_rope_axis(x[..., :r], row), _rope_axis(x[..., r:], col)], axis=-1)

def map_query_blocks(fn, q):
    b, l = q.shape[:2]
    nb = l // QBLOCK
    qb = jnp.moveaxis(q.reshape((b, nb, QBLOCK) + q.shape[2:]), 1, 0)
    out = jnp.moveaxis(lax.map(fn, qb), 0, 1)
    return out.reshape((b, l) + out.shape[3:])

def modulation(cond, w_mod, b_mod):
    m = jax.nn.silu(cond) @ w_mod + b_mod
    return jnp.split(m[..., None, :], 6, axis=-1)

def retention_scan(q, k, v, log_gamma, s0):
    b, l, h, _ = q.shape
    dv = v.shape[-1]
    n = l // RET_CHUNK

    def chunks(t):
        return t.astype(jnp.float32).reshape(b, n, RET_CHUNK, h, t.shape[-1]).transpose(1, 0, 3, 2, 4)

    idx = jnp.arange(RET_CHUNK, dtype=jnp.float32)
    dist = idx[:, None] - idx[None, :]
    lg = log_gamma.astype(jnp.float32)
    intra = jnp.where(dist >= 0, jnp.exp(lg[:, None, None] * jnp.maximum(dist, 0.0)), 0.0)
    q_dec = jnp.exp(lg[:, None] * (idx + 1.0))[None, :, :, None]
    k_dec = jnp.exp(lg[:, None] * (RET_CHUNK - 1.0 - idx))[None, :, :, None]
    c_dec = jnp.exp(lg * RET_CHUNK)[None, :, None, None]

    def step(s, blk):
        qc, kc, vc = blk
        scores = jnp.einsum('bhqd,bhkd->bhqk', qc, kc) * intra
        o = jnp.einsum('bhqk,bhke->bhqe', scores, vc) + jnp.einsum('bhqd,bhde->bhqe', qc, s) * q_dec
        s = s * c_dec + jnp.einsum('bhkd,bhke->bhde', kc * k_dec, vc)
        return s, o

    s_fin, o = lax.scan(step, s0.astype(jnp.float32), (chunks(q), chunks(k) * (RET_DK ** -0.5), chunks(v)))
    return o.transpose(1, 0, 3, 2, 4).reshape(b, l, h, dv), s_fin

def bidir_retention(q, k, v, g, decay_logit, s0):
    log_gamma = jax.nn.log_sigmoid(decay_logit.astype(jnp.float32))
    o_f, s_f = retention_scan(q, k, v, log_gamma[0], s0[:, 0])
    o_b, s_b = retention_scan(jnp.flip(q, 1), jnp.flip(k, 1), jnp.flip(v, 1), log_gamma[1], s0[:, 1])
    o = head_layernorm(o_f + jnp.flip(o_b, 1))
    b, l = q.shape[:2]
    o = o.reshape(b, l, -1).astype(g.dtype) * jax.nn.silu(g)
    return o, jnp.stack([s_f, s_b], axis=1)

def sink_attention_context(q, k, v, sink):
    b, _, hq, hd = q.shape
    g = k.shape[2]
    r = hq // g
    sink_logit = sink.astype(jnp.float32).reshape(g, r)
    scale = hd ** -0.5

    def block(qb):
        qb = qb.reshape(b, QBLOCK, g, r, hd)
        s = jnp.einsum('bqgrd,bkgd->bgrqk', qb, k).astype(jnp.float32) * scale
        sk = jnp.broadcast_to(sink_logit[None, :, :, None, None], s.shape[:-1] + (1,))
        p = jax.nn.softmax(jnp.concatenate([s, sk], axis=-1), axis=-1)[..., :-1]
        return jnp.einsum('bgrqk,bkgd->bqgrd', p.astype(v.dtype), v).reshape(b, QBLOCK, hq * hd)

    return map_query_blocks(block, q)

def window_attention(q, k, v, kc, vc, sink):
    b, n_tok, hq, hd = q.shape
    g = k.shape[2]
    r = hq // g
    m = kc.shape[1]
    nb = n_tok // WIN_BLOCK
    w = WIN_BLOCK
    qb = q.reshape(b, nb, w, g, r, hd)

    def neighbours(t):
        tp = jnp.pad(t, ((0, 0), (w, w), (0, 0), (0, 0))).reshape(b, nb + 2, w, g, hd)
        return jnp.concatenate([tp[:, :-2], tp[:, 1:-1], tp[:, 2:]], axis=2)

    kn, vn = neighbours(k), neighbours(v)
    blk = jnp.arange(nb)[:, None]
    qpos = blk * w + jnp.arange(w)[None, :]
    kpos = blk * w - w + jnp.arange(3 * w)[None, :]
    mask = (jnp.abs(qpos[:, :, None] - kpos[:, None, :]) <= WINDOW) & ((kpos >= 0) & (kpos < n_tok))[:, None, :]
    scale = hd ** -0.5
    s_lat = jnp.einsum('bnqgrd,bnkgd->bngrqk', qb, kn).astype(jnp.float32) * scale
    s_lat = jnp.where(mask[None, :, None, None], s_lat, NEG_INF)
    s_ctx = jnp.einsum('bnqgrd,bmgd->bngrqm', qb, kc).astype(jnp.float32) * scale
    s_sink = jnp.broadcast_to(sink.astype(jnp.float32).reshape(g, r)[None, None, :, :, None, None], s_lat.shape[:-1] + (1,))
    p = jax.nn.softmax(jnp.concatenate([s_lat, s_ctx, s_sink], axis=-1), axis=-1)
    p_lat = p[..., :3 * w].astype(v.dtype)
    p_ctx = p[..., 3 * w:3 * w + m].astype(v.dtype)
    o = jnp.einsum('bngrqk,bnkgd->bnqgrd', p_lat, vn) + jnp.einsum('bngrqm,bmgd->bnqgrd', p_ctx, vc)
    return o.reshape(b, n_tok, hq * hd)

def diff_attention(q, k, v, lam):
    scale = DIFF_D ** -0.5

    def block(qb):
        s = jnp.einsum('bqhcd,bkhcd->bhcqk', qb, k).astype(jnp.float32) * scale
        p = jax.nn.softmax(s, axis=-1)
        a = p[:, :, 0] - lam * p[:, :, 1]
        return jnp.einsum('bhqk,bkhe->bqhe', a.astype(v.dtype), v)

    return map_query_blocks(block, q)

def mla_attention(q, k_nope, k_rope, v):
    scale = (MLA_NOPE + MLA_ROPE) ** -0.5

    def block(qb):
        s = jnp.einsum('bqhd,bkhd->bhqk', qb[..., :MLA_NOPE], k_nope) + jnp.einsum('bqhd,bkd->bhqk', qb[..., MLA_NOPE:], k_rope)
        p = jax.nn.softmax(s.astype(jnp.float32) * scale, axis=-1)
        return jnp.einsum('bhqk,bkhe->bqhe', p.astype(v.dtype), v)

    return map_query_blocks(block, q)

def trunk_layer(x, cond, p, lam_init, ctx):
    b, l, _ = x.shape
    latent = ctx is not None
    shift1, scale1, gate1, shift2, scale2, gate2 = modulation(cond, p['w_mod'], p['b_mod'])
    h = rmsnorm(x, p['g_mix']) * (1 + scale1) + shift1
    cuts = [int(cc) for cc in np.cumsum(IN_SPLITS)[:-1]]
    (rq, rk, rv, rg, wq, wk, wv, dq, dk, dv, mcq, mckv, mkr) = jnp.split(h @ p['w_in'], cuts, axis=-1)

    rq = rq.reshape(b, l, RET_H, RET_DK)
    rk = rk.reshape(b, l, RET_H, RET_DK)
    rv = rv.reshape(b, l, RET_H, RET_DV)
    s0 = ctx[0] if latent else jnp.zeros((b, 2, RET_H, RET_DK, RET_DV), jnp.float32)
    o_ret, ret_state = bidir_retention(rq, rk, rv, rg, p['ret_decay'], s0)

    wq = wq.reshape(b, l, WIN_HQ, WIN_HD)
    wk = wk.reshape(b, l, WIN_HKV, WIN_HD)
    wv = wv.reshape(b, l, WIN_HKV, WIN_HD)
    if latent:
        o_win = window_attention(rope_2d(wq), rope_2d(wk), wv, ctx[1], ctx[2], p['win_sink'])
    else:
        o_win = sink_attention_context(wq, wk, wv, p['win_sink'])

    dl = p['diff_lambda'].astype(jnp.float32)
    lam = jnp.exp(jnp.sum(dl[0] * dl[1])) - jnp.exp(jnp.sum(dl[2] * dl[3])) + lam_init
    dk_flat = dk.reshape(b, l, DIFF_H, 2 * DIFF_D)
    dv_h = dv.reshape(b, l, DIFF_H, DIFF_DV)
    if latent:
        dq_h = rope_2d(dq.reshape(b, l, 2 * DIFF_H, DIFF_D)).reshape(b, l, DIFF_H, 2, DIFF_D)
        dk_lat = rope_2d(dk.reshape(b, l, 2 * DIFF_H, DIFF_D)).reshape(b, l, DIFF_H, 2, DIFF_D)
        dk_all = jnp.concatenate([dk_lat, ctx[3].reshape(b, -1, DIFF_H, 2, DIFF_D)], axis=1)
        dv_all = jnp.concatenate([dv_h, ctx[4]], axis=1)
    else:
        dq_h = dq.reshape(b, l, DIFF_H, 2, DIFF_D)
        dk_all = dk.reshape(b, l, DIFF_H, 2, DIFF_D)
        dv_all = dv_h
    o_diff = diff_attention(dq_h, dk_all, dv_all, lam)
    o_diff = (rmsnorm(o_diff, p['g_diff']) * (1.0 - lam_init)).reshape(b, l, DIFF_H * DIFF_DV)

    mq = (rmsnorm(mcq, p['g_mla_q']) @ p['w_mla_uq']).reshape(b, l, MLA_H, MLA_NOPE + MLA_ROPE)
    ckv = rmsnorm(mckv, p['g_mla_kv'])
    kv = (ckv @ p['w_mla_ukv']).reshape(b, l, MLA_H, MLA_NOPE + MLA_V)
    if latent:
        mq = jnp.concatenate([mq[..., :MLA_NOPE], rope_2d(mq[..., MLA_NOPE:])], axis=-1)
        kr_lat = rope_2d(mkr[:, :, None, :])[:, :, 0]
        kv_ctx = (ctx[5] @ p['w_mla_ukv']).reshape(b, -1, MLA_H, MLA_NOPE + MLA_V)
        kv_all = jnp.concatenate([kv, kv_ctx], axis=1)
        kr_all = jnp.concatenate([kr_lat, ctx[6]], axis=1)
    else:
        kv_all = kv
        kr_all = mkr
    o_mla = mla_attention(mq, kv_all[..., :MLA_NOPE], kr_all, kv_all[..., MLA_NOPE:]).reshape(b, l, MLA_H * MLA_V)

    branches = jnp.stack([o_ret, o_win, o_diff, o_mla], axis=2)
    branches = jnp.einsum('blnc,ncd->blnd', branches, p['w_branch'])
    gates = jax.nn.sigmoid((h @ p['w_gate'] + p['b_gate']).reshape(b, l, N_BRANCH, D_MODEL))
    mixed = jnp.sum(gates * branches, axis=2) @ p['w_out']
    x = x + gate1 * mixed

    h2 = rmsnorm(x, p['g_ffn']) * (1 + scale2) + shift2
    u = h2 @ p['w_up'] + p['b_up']
    pad = CONV_W // 2
    up = jnp.pad(u, ((0, 0), (pad, pad), (0, 0)))
    conv = p['b_conv']
    for j in range(CONV_W):
        conv = conv + p['w_conv'][j] * up[:, j:j + l]
    a, gg = jnp.split(conv, 2, axis=-1)
    x = x + gate2 * ((jax.nn.silu(gg) * a) @ p['w_down'])

    if latent:
        return x, None
    return x, (ret_state, wk, wv, dk_flat, dv_h, ckv, mkr)

def setup_inputs(seed: int = 0) -> dict:
    key = jax.random.key(seed)
    ks = iter(jax.random.split(key, 48))

    def nrm(shape, scale):
        return jax.random.normal(next(ks), shape, jnp.float32) * scale

    def gain(shape):
        return 1.0 + nrm(shape, 0.1)

    gamma = 1.0 - 2.0 ** (-5.0 - np.arange(RET_H))
    decay_base = jnp.asarray(np.log(gamma / (1.0 - gamma)).astype(np.float32))
    d = D_MODEL
    return {
        'x_prompt': nrm((BATCH, SEQ, d), 1.0),
        'x_sample': nrm((DEC_BATCH, DEC_SEQ, d), 1.0),
        'state_ret': nrm((DEC_BATCH, DEPTH, 2, RET_H, RET_DK, RET_DV), 1.0),
        'cache_win_k': nrm((DEC_BATCH, DEPTH, PAST_LEN, WIN_HKV, WIN_HD), 1.0),
        'cache_win_v': nrm((DEC_BATCH, DEPTH, PAST_LEN, WIN_HKV, WIN_HD), 1.0),
        'cache_diff_k': nrm((DEC_BATCH, DEPTH, PAST_LEN, DIFF_H, 2 * DIFF_D), 1.0),
        'cache_diff_v': nrm((DEC_BATCH, DEPTH, PAST_LEN, DIFF_H, DIFF_DV), 1.0),
        'cache_mla_ckv': nrm((DEC_BATCH, DEPTH, PAST_LEN, MLA_KVRANK), 1.0),
        'cache_mla_krope': nrm((DEC_BATCH, DEPTH, PAST_LEN, MLA_ROPE), 1.0),
        'c': nrm((DEC_BATCH, d), 1.0),
        'c_ctx': nrm((d,), 1.0),
        'w_mod': nrm((DEPTH, d, 6 * d), 0.5 * d ** -0.5),
        'b_mod': nrm((DEPTH, 6 * d), 0.02),
        'g_mix': gain((DEPTH, d)),
        'w_in': nrm((DEPTH, d, IN_WIDTH), d ** -0.5),
        'ret_decay': decay_base[None, None, :] + nrm((DEPTH, 2, RET_H), 0.1),
        'win_sink': nrm((DEPTH, WIN_HQ), 0.5),
        'diff_lambda': nrm((DEPTH, 4, DIFF_D), 0.1),
        'g_diff': gain((DEPTH, DIFF_DV)),
        'g_mla_q': gain((DEPTH, MLA_QRANK)),
        'w_mla_uq': nrm((DEPTH, MLA_QRANK, MLA_H * (MLA_NOPE + MLA_ROPE)), MLA_QRANK ** -0.5),
        'g_mla_kv': gain((DEPTH, MLA_KVRANK)),
        'w_mla_ukv': nrm((DEPTH, MLA_KVRANK, MLA_H * (MLA_NOPE + MLA_V)), MLA_KVRANK ** -0.5),
        'w_branch': nrm((DEPTH, N_BRANCH, BRANCH_W, d), BRANCH_W ** -0.5),
        'w_gate': nrm((DEPTH, d, N_BRANCH * d), d ** -0.5),
        'b_gate': nrm((DEPTH, N_BRANCH * d), 0.02),
        'w_out': nrm((DEPTH, d, d), d ** -0.5),
        'g_ffn': gain((DEPTH, d)),
        'w_up': nrm((DEPTH, d, 2 * D_FF), d ** -0.5),
        'b_up': nrm((DEPTH, 2 * D_FF), 0.02),
        'w_conv': nrm((DEPTH, CONV_W, 2 * D_FF), CONV_W ** -0.5),
        'b_conv': nrm((DEPTH, 2 * D_FF), 0.02),
        'w_down': nrm((DEPTH, D_FF, d), D_FF ** -0.5),
        'g_final': gain((d,)),
    }

def reference(x_prompt, x_sample, state_ret, cache_win_k, cache_win_v, cache_diff_k, cache_diff_v, cache_mla_ckv, cache_mla_krope, c, c_ctx, w_mod, b_mod, g_mix, w_in, ret_decay, win_sink, diff_lambda, g_diff, g_mla_q, w_mla_uq, g_mla_kv, w_mla_ukv, w_branch, w_gate, b_gate, w_out, g_ffn, w_up, b_up, w_conv, b_conv, w_down, g_final):
    xp = x_prompt
    xs = x_sample
    produced = [[] for _ in range(7)]
    for li in range(DEPTH):
        p = {'w_mod': w_mod[li], 'b_mod': b_mod[li], 'g_mix': g_mix[li], 'w_in': w_in[li],
             'ret_decay': ret_decay[li], 'win_sink': win_sink[li], 'diff_lambda': diff_lambda[li],
             'g_diff': g_diff[li], 'g_mla_q': g_mla_q[li], 'w_mla_uq': w_mla_uq[li],
             'g_mla_kv': g_mla_kv[li], 'w_mla_ukv': w_mla_ukv[li], 'w_branch': w_branch[li],
             'w_gate': w_gate[li], 'b_gate': b_gate[li], 'w_out': w_out[li], 'g_ffn': g_ffn[li],
             'w_up': w_up[li], 'b_up': b_up[li], 'w_conv': w_conv[li], 'b_conv': b_conv[li],
             'w_down': w_down[li]}
        lam_init = 0.8 - 0.6 * math.exp(-0.3 * li)
        xp, ctx_new = trunk_layer(xp, c_ctx, p, lam_init, None)
        for lst, t in zip(produced, ctx_new):
            lst.append(t)
        ctx_cached = (state_ret[:, li], cache_win_k[:, li], cache_win_v[:, li], cache_diff_k[:, li],
                      cache_diff_v[:, li], cache_mla_ckv[:, li], cache_mla_krope[:, li])
        xs, _ = trunk_layer(xs, c, p, lam_init, ctx_cached)
    y_prompt = rmsnorm(xp, g_final)
    y_sample = rmsnorm(xs, g_final)
    new_state_ret = jnp.stack(produced[0], axis=1)
    new_cache_win_k = jnp.stack(produced[1], axis=1)
    new_cache_win_v = jnp.stack(produced[2], axis=1)
    new_cache_diff_k = jnp.stack(produced[3], axis=1)
    new_cache_diff_v = jnp.stack(produced[4], axis=1)
    new_cache_mla_ckv = jnp.stack(produced[5], axis=1)
    new_cache_mla_krope = jnp.stack(produced[6], axis=1)
    return (y_prompt, y_sample, new_state_ret, new_cache_win_k, new_cache_win_v, new_cache_diff_k, new_cache_diff_v, new_cache_mla_ckv, new_cache_mla_krope)


_drawn_inputs = setup_inputs


def setup_inputs(seed=0):
    import zlib

    import numpy as np

    out = dict(_drawn_inputs(seed))
    spreads = {}
    factors = {'cache_win_k': 5.076,
     'cache_win_v': 4.232,
     'cache_mla_ckv': 7.94,
     'cache_mla_krope': 8.0,
     'win_sink': 8.0,
     'diff_lambda': 8.0,
     'g_mla_q': 8.0,
     'b_gate': 8.0,
     'b_up': 7.357,
     'b_conv': 7.35}
    for name, (base, spread) in spreads.items():
        noise = np.random.default_rng([zlib.crc32(name.encode()), seed]).standard_normal(out[name].shape)
        drawn = base * np.exp(spread * noise) if base else spread * noise
        out[name] = jnp.asarray(drawn.astype(out[name].dtype))
    for name, factor in factors.items():
        out[name] = (out[name] * factor).astype(out[name].dtype)
    return out
```

```python
import math
from contextlib import ExitStack

import numpy as np

import concourse.bass as bass
from concourse import mybir

F32 = mybir.dt.float32
F32R = mybir.dt.float32r
ACT = mybir.ActivationFunctionType
ALU = mybir.AluOpType
AX = mybir.AxisListType

P = 128
D = 1024
KD = D // P
DEPTH = 2
CTX = 128
LAT = 512
TOK = CTX + LAT
T = TOK // P
NL = LAT // P
HALF = TOK // 2
PAST = 128
KEYS = TOK + PAST
GRID_W = 64
EPS = 1e-6
NEG = -1e30
D_FF = 2816
FFT = D_FF // P
BW = 256
IN_W = 2720
NB = 4
SCALES = {1: 64 ** -0.5, 2: 32 ** -0.5, 3: 96 ** -0.5}
BANK = 512
PADDED = TOK + 2
UB = PADDED + 2
LAM0 = 0.8 - 0.6
LAM_DECAY = math.exp(-0.3)

G_COLS = [(0, 512), (512, 512), (1024, 512), (1536, 512), (2048, 512), (2560, 160)]
UP_GROUPS = [(0, 8), (8, 8), (16, 6)]
ACT_SLOTS = 12

CONST_COLS = dict(ident=P, fold=2, mprev=P, mnext=P, dpos=P, upf=P, dneg=P, upb=P, rowf=P, rowb=P, colf=1, colb=1,
                  c16=NL * 64, s16=NL * 64, c8=NL * 32, s8=NL * 32)


def const_at():
    at, where = 0, {}
    for name, n in CONST_COLS.items():
        where[name] = (at, n)
        at += n
    return where, at


def shape_constants():
    where, n = const_at()
    out = np.zeros((P, n), np.float32)

    def put(name, a):
        out[:, where[name][0]:where[name][0] + where[name][1]] = np.asarray(a, np.float32).reshape(P, -1)

    i = np.arange(P)
    row, col = i[:, None], i[None, :]
    put("ident", row == col)
    put("fold", i[:, None] % 2 == np.arange(2))
    put("mprev", np.where(col >= row, 0.0, NEG))
    put("mnext", np.where(col <= row, 0.0, NEG))
    put("dpos", np.maximum(col - row, 0))
    put("upf", col >= row)
    put("dneg", np.maximum(row - col, 0))
    put("upb", row >= col)
    put("rowf", np.broadcast_to(i + 1, (P, P)))
    put("rowb", np.broadcast_to(P - i, (P, P)))
    put("colf", P - 1 - i)
    put("colb", i)
    n_tok = np.arange(LAT).reshape(NL, P).T
    for w, c, s in ((16, "c16", "s16"), (8, "c8", "s8")):
        freqs = np.float32(10000.0) ** (-np.arange(w, dtype=np.float32) / np.float32(w))
        ang = np.stack([(n_tok // GRID_W)[..., None] * freqs, (n_tok % GRID_W)[..., None] * freqs], 2)
        ang = ang.astype(np.float32)[:, :, :, None, :]
        put(c, np.concatenate([np.cos(ang), np.cos(ang)], 3))
        put(s, np.concatenate([-np.sin(ang), np.sin(ang)], 3))
    return out


def weight_units():
    mod = iter(range(24))
    win = lambda g: [("in", (g, half), True) for half in range(2)]
    mods = lambda n: [("mod", next(mod), True) for _ in range(n)]
    units = mods(8) + win(0) + win(1) + win(2) + mods(5) + win(3) + win(4) + mods(5) + win(5)
    units += [("uq", 0, False), ("ukv", 0, False)] + mods(6)
    for mp in range(4):
        units += [("gate", (mp, n), True) for n in range(NB)]
    units += [("out", mp, True) for mp in range(4)]
    for g, (j0, nj) in enumerate(UP_GROUPS):
        units += [("up", j, True) for j in range(j0, j0 + nj)] + [("down", (g, mp), True) for mp in range(4)]
    return units


UNITS = weight_units()
N_UNITS = len(UNITS)
N_SPLIT = sum(split for _, _, split in UNITS)
RAW = 3
WS = 2


def unit_loads(u):
    return 2 if UNITS[u][0] == "up" else 1


def loaded_count(u):
    return 16 * sum(unit_loads(v) for v in range(u % RAW, u + 1, RAW))



HEADS = [(br, t, h) for br in (1, 2, 3) for t in range(T) for h in range(4)]
MAPS = []
for a, (br, t, h) in enumerate(HEADS):
    MAPS += [(a, c) for c in range(2 if br == 2 else 1)]
FIRST_MAP = [next(m for m, (b, _) in enumerate(MAPS) if b == a) for a in range(len(HEADS))]
N_MAPS, N_HEADS = len(MAPS), len(HEADS)


def window_blocks(t):
    if t == 0:
        return [(0, None)]
    near = [(b, "mprev" if b < t else "mnext" if b > t else None) for b in (t - 1, t, t + 1) if 1 <= b <= NL]
    return near + [(T, None)]


def key_blocks(br, t):
    if br == 1:
        return [b for b, _ in window_blocks(t)]
    return [0] if t == 0 else list(range(1, T + 1))


def build(nc, a, outs):
    (y_prompt, y_sample, o_state, o_win_k, o_win_v, o_diff_k, o_diff_v, o_ckv, o_krope) = outs
    where, n_const = const_at()
    ctx = ExitStack()
    with ctx:
        slab = nc.alloc_sbuf_tensor("slab", [P, (nc.sbuf_usable_end - 1344) // 4], F32)
        top = [1536]

        def at(name, shape, dtype=F32, offset=None):
            size = int(np.prod(shape[1:])) * 4
            if offset is None:
                offset = top[0]
                top[0] += (size + 31) // 32 * 32
            assert offset + size <= nc.sbuf_usable_end - 64, (name, offset + size)
            return nc.alloc_sbuf_tensor_at(name, shape, dtype, offset=offset)

        x = at("x", [P, KD, TOK])
        h_hi, h_lo = at("h_hi", [P, KD, TOK], F32R), at("h_lo", [P, KD, TOK], F32R)
        raw = [at(f"raw{i}", [P, 2048]) for i in range(RAW)]
        w_hi = [at(f"w_hi{i}", [P, 2048], F32R) for i in range(WS)]
        w_lo = [at(f"w_lo{i}", [P, 2048], F32R) for i in range(WS)]
        const = at("const", [P, n_const])
        ones = at("ones", [P, P])
        vcol = at("vcol", [P, 316])
        dden = at("dden", [P, 2, 4])
        orec = at("orec", [P, 4])
        cond = at("cond", [P, 16])
        cond_r = at("cond_r", [P, KD, 4], F32R)
        mod = at("mod", [P, 48, 2])
        scl = at("scl", [P, 2, KD, 2])
        CACHE = top[0]
        cache = at("cache", [P, 928])
        state0 = at("state0", [P, 2, 2, 64])
        decay = at("decay", [P, 12])
        lgam = at("lgam", [P, 12])
        dec_t = at("dec_t", [P, 4, 12])
        kdec = at("kdec", [P, 2, 4])
        cdec = at("cdec", [P, 4])
        sink = at("sink", [P, 4])
        dlam = at("dlam", [P, 4, 32])
        dsum = at("dsum", [P, 4])
        lam = at("lam", [P, 1])
        lam_init = at("lam_init", [P, 1])
        one_minus = at("one_minus", [P, 1])
        g_diff = at("g_diff", [P, 64])
        gd = at("gd", [P, 64])
        g_mq = at("g_mq", [P, BW])
        g_mkv = at("g_mkv", [P, P])
        st5 = at("st5", [P, 4, 20])
        stat = at("stat", [P, 7, 8])
        eps_c = at("eps_c", [P, 1])
        token = at("token", [P, 1])
        BASE = (top[0] + 31) // 32 * 32
        Z0, Z1, TMP, PR, PTR, OR, FM, OTR = (BASE + b for b in (0, 10240, 20480, 26624, 36864, 41984, 47104, 69632))
        NT = BASE + 53760

        z = [at("z0", [P, T, 512], offset=Z0), at("z1", [P, T, 512], offset=Z1)]
        z5 = at("z5", [P, T, 160], offset=Z0)
        z_mq = at("z_mq", [P, T, 384], offset=Z1)
        v_mla = at("v_mla", [P, T + 1, BW], offset=Z0 + T * 160 * 4)
        rope_tmp = {1: at("rope1", [P, NL, 384], offset=TMP), 2: at("rope2", [P, NL, 512], offset=FM + 12288),
                    3: at("rope3", [P, NL, 4, 32], offset=TMP), 4: at("rope4", [P, NL, 1, 32], offset=TMP + 2048)}
        dprod = at("dprod", [P, 2, 32], offset=TMP + 4096)
        post = at("post", [P, T, BW], offset=TMP)
        decay_f = at("decay_f", [P, 4, P], offset=TMP)
        decay_b = at("decay_b", [P, 4, P], offset=TMP + 2048)
        probs = at("probs", [P, 4, TOK], offset=PR)
        probs_t = at("probs_t", [P, 2, T, P], offset=PTR)
        o_tm = at("o_tm", [P, T, BW], offset=OR)
        sq_kv = at("sq_kv", [P, T, P], offset=PTR)
        rqk = at("rqk", [P, 4, TOK], offset=FM)
        dmask = at("dmask", [P, 4, P], offset=FM + 10240)
        qdec = at("qdec", [P, 4, P], offset=FM + 12288)
        kd = at("kd", [P, 2, 8, 64], offset=FM + 14336)
        states = at("states", [P, 2, NL, 2, 64], offset=FM + 18432)
        st_dec = at("st_dec", [P, 2, 4, P], offset=PR)
        q_dec = at("q_dec", [P, 2, 4, P], offset=PR + 4096)
        state_c = at("state_c", [P, 4, 64], offset=PR + 8192)
        wq_t, wk_t = at("wq_t", [P, 2, TOK], offset=FM), at("wk_t", [P, 2, KEYS], offset=FM + 5120)
        dq_t, dk_t = at("dq_t", [P, 2, TOK], offset=FM), at("dk_t", [P, 2, KEYS], offset=FM + 5120)
        mq_t, mk_t = at("mq_t", [P, 4, TOK], offset=FM), at("mk_t", [P, 4, KEYS], offset=FM + 10240)
        cq_t, ckv_t = at("cq_t", [P, 2, TOK], offset=PR), at("ckv_t", [P, KEYS], offset=PR + 5120)
        o_t = at("o_t", [P, 8, TOK], offset=OTR)
        rows = at("rows", [P, 4, P], offset=OTR + 7 * TOK * 4)
        mod_row = at("mod_row", [P, 2, 256], offset=OTR + 7 * TOK * 4)
        mix_hi = at("mix_hi", [P, KD, TOK], F32R, offset=BASE)
        mix_lo = at("mix_lo", [P, KD, TOK], F32R, offset=BASE + 20480)
        w_br = [at("w_br0", [P, 8, 256], offset=BASE + 49152), at("w_br1", [P, 8, 256], offset=BASE + 40960)]
        sig = at("sig", [P, 2, TOK], offset=BASE + 57344)
        acc = at("acc", [P, 2, TOK], offset=BASE + 62464)
        gprod = at("gprod", [P, TOK], offset=CACHE)
        sq = at("sq", [P, TOK], offset=BASE + 82272)
        ss = at("ss", [P, TOK], offset=BASE + 84832)
        t1 = at("t1", [P, 2, TOK], offset=NT + 5120)
        hf = at("hf", [P, 2, TOK], offset=NT + 10240)
        diag = at("diag", [P, T, P], offset=NT + 15360)
        a_hi = at("a_hi", [P, ACT_SLOTS, PADDED], F32R, offset=BASE)
        a_lo = at("a_lo", [P, ACT_SLOTS, PADDED], F32R, offset=BASE + 30816)
        FB = BASE + 61632
        u_pad = at("u_pad", [P, 2, 2, UB], offset=FB)
        conv = at("conv", [P, 2, PADDED], offset=FB + 10304)
        usig = at("usig", [P, PADDED], offset=FB + 15456)
        act = at("act", [P, PADDED], offset=FB + 18048)
        x_tm = at("x_tm", [P, T, D], offset=BASE)
        y_tm = at("y_tm", [P, T, D], offset=BASE + 20480)
        g_fin = at("g_fin", [P, D], offset=BASE + 40960)
        crow = at("crow", [16, P], offset=BASE + 49152)

        def c(name, lo=0, hi=None):
            s, n = where[name]
            return const[:, s + lo:s + (n if hi is None else hi)]

        ident = c("ident")
        ps = ctx.enter_context(nc.psum_tensor("ps", [P, 8 * BANK], F32))

        def state_of(r, n):
            return state0[:, r] if n == (0, NL - 1)[r] else states[:, r, n]

        def bank(b, lo=0, hi=BANK):
            return ps[:, b * BANK + lo:b * BANK + hi]

        def mod_col(i):
            return (7 if i >= 8 else 1 + 2 * (i % 2)) * BANK

        def mod_t_col(i):
            return 5 * BANK if i < 8 else 6 * BANK + 256

        def tok2(b):
            return ps[:, b * BANK:(b + 2) * BANK].rearrange("p (a n) -> p a n", a=2)[:, :, 0:HALF]

        def two(ap):
            return ap.rearrange("p (a n) -> p a n", a=2)

        BMOD, GMIX, GFFN, BGATE, BUP, BCONV, WCONV = 0, 48, 56, 64, 96, 140, (184, 228, 272)

        class Signal:

            def __init__(self, name, per_layer=1):
                self.sem, self.per = ctx.enter_context(nc.semaphore(name)), per_layer

        raw_loaded = [Signal(f"raw_loaded{i}", loaded_count(max(range(i, N_UNITS, RAW)))) for i in range(RAW)]
        hi_done, lo_done = Signal("w_high_ready", N_SPLIT), Signal("w_low_ready", N_SPLIT - 8)
        v_lo_done = Signal("w_low_by_vector", 8)
        raw_free = Signal("raw_free")
        half_mm, gatew_mm = Signal("in_first_half", 6), Signal("gate_weights_used", 16)
        N_SMALL = 25
        small = Signal("small_loaded", 16 * N_SMALL)
        start_loaded, made = Signal("start_loaded"), Signal("constants_made")
        cond_t, cond_raw, cond_sig, cond_done = (Signal(n) for n in ("cond_t", "cond_raw", "cond_sigmoid", "cond_ready"))
        xin_t, xin_done = Signal("x_transposed"), Signal("x_ready")
        vec_t, vec_done = Signal("vectors_transposed"), Signal("vectors_ready")
        mod_mm, row_done, mod_t = (Signal(n, 24) for n in ("mod_product", "mod_row_ready", "mod_transposed"))
        mod_done, scl_done = Signal("mod_ready", 24), Signal("scale_ready", 2)
        ss_done = [Signal("squares_ready0"), Signal("squares_ready1")]
        ss_mm = Signal("square_sums", 2)
        rms_done, diag_done, bc_mm = Signal("rms_ready", 2), Signal("rstd_diagonal", 2), Signal("rstd_spread", 2)
        t1_done, hf_done, hh_done, h_done = (Signal(n, 16) for n in ("normed", "h_full", "h_high", "h_ready"))
        z_mm, z_done = Signal("in_product", 6 * T), Signal("z_ready", 6 * T)
        branch_loaded = [Signal(f"branch_loaded{i}", 32) for i in range(2)]
        cache_out = Signal("cache_written", 16 * 10)
        tab_arg, tab_exp = Signal("decay_arguments", 2), Signal("decay_exponents", 2)
        kdec_done, dmask_done = Signal("key_decay_ready"), Signal("decay_mask_ready")
        rt_mm, rt_done = Signal("ret_transposed", T), Signal("ret_qk_ready", T)
        kd_done, u_mm = Signal("keys_decayed", T), Signal("state_products", T)
        st_out, s_done = Signal("context_state"), Signal("states_ready")
        rs_mm, rst_done = Signal("ret_scores", T), Signal("ret_decayed", 2 * T)
        ro_mm, ro_done = Signal("ret_out_product", T), Signal("ret_out_ready", T)
        post_in, post_act = Signal("post_for_scalar", 4), Signal("post_by_scalar", 5)
        ret_o, diff_o = Signal("ret_normed"), Signal("diff_normed")
        ot_mm, ot_done = Signal("o_transposed", 8), Signal("o_t_ready", 8)
        rope_done = Signal("roped", 3)
        qk_mm, qk_done = Signal("qk_transposed", 7), Signal("qk_ready", 7)
        s_mm, bias_done, exp_done = Signal("scores", N_MAPS), Signal("softmax_bias", N_MAPS), Signal("exponents", N_MAPS)
        comb_done = Signal("maps_combined", 4 * T)
        pt_mm, pt_done = Signal("probs_transposed", N_HEADS), Signal("probs_t_ready", N_HEADS)
        pv_mm, oev_done = Signal("pv_product", N_HEADS), Signal("head_out", 3 * T)
        prep_in, prep_act, prep_done = Signal("mla_sums", 2), Signal("mla_by_scalar", 4), Signal("mla_normed")
        MLA_ITEMS = 4 + T + 4 + (T + 1) + 4
        mla_mm, mla_done = Signal("mla_product", MLA_ITEMS), Signal("mla_ready", MLA_ITEMS)
        gate_mm, gate_sig, gate_read = Signal("gate_product", 32), Signal("gate_sigmoid", 32), Signal("gate_read", 32)
        mix_acc, mix_h, mix_done = Signal("mixed_sum", 8), Signal("mixed_high", 8), Signal("mixed_ready", 8)
        out_mm, x_out = Signal("out_product", 8), Signal("x_after_mixers", 8)
        pads_done = Signal("pads_zeroed")
        up_mm, up_done = Signal("up_product", FFT), Signal("up_ready", FFT)
        cv_done, sg_done, af_done = Signal("conv_ready", FFT), Signal("mlp_sigmoid", FFT), Signal("mlp_product", FFT)
        ah_done, al_done = Signal("act_high", FFT), Signal("act_ready", FFT)
        down_mm, x_down = Signal("down_product", 24), Signal("x_after_mlp", 24)
        gfin, yt_mm, yss_mm, yst_done, yrec, y_done, y_out = (Signal(n) for n in (
            "g_final_loaded", "y_transposed", "y_square_sums", "y_rms", "y_rstd", "y_ready", "y_written"))
        vstep, vstart = Signal("vector_step"), Signal("vector_start")

        def counts(li):
            def now(sig, k):
                assert k > 0
                return li * sig.per + k
            return now

        class Steps:

            def __init__(self, base):
                self.base, self.n = base, 0

            def __call__(self):
                self.n += 1
                return self.base + self.n

        def query(br, t, h, m):
            cols = slice(t * P, t * P + P)
            if br == 1:
                return wq_t[64 * (h % 2):64 * (h % 2) + 64, h // 2, cols]
            if br == 2:
                p0 = 64 * (h % 2) + 32 * m
                return dq_t[p0:p0 + 32, h // 2, cols]
            return mq_t[0:96, h, cols]

        def keys(br, h, m, k0, n):
            if br == 1:
                return wk_t[64 * (h % 2):64 * (h % 2) + 64, h // 2, k0:k0 + n]
            if br == 2:
                p0 = 64 * (h % 2) + 32 * m
                return dk_t[p0:p0 + 32, h // 2, k0:k0 + n]
            return mk_t[0:96, h, k0:k0 + n]

        def values(br, b, h):
            if br == 1:
                c0 = 64 * (h // 2)
                return z[0][:, b, 384 + c0:448 + c0] if b < T else cache[:, 128 + c0:192 + c0]
            if br == 2:
                return z[1][:, b, 64 * h:64 * h + 64] if b < T else cache[:, 512 + 64 * h:576 + 64 * h]
            return v_mla[:, b, 64 * h:64 * h + 64]

        def pt_bank(br, a_):
            return 4 + a_ % 2 if br == 1 else 4

        def score_runs(blocks):
            runs = []
            for i, b in enumerate(blocks):
                if runs and runs[-1][1] + runs[-1][2] == b * P and (i * P) % BANK:
                    runs[-1][2] += P
                else:
                    runs.append([i * P, b * P, P])
            return runs

        MOD_STEPS = {1: (2, 4, 7, 10, 14), 2: (2, 4, 7, 10, 14), 3: (2, 4, 6, 8, 11, 14)}
        STEPS = 4 * T + 3

        block = ctx.enter_context(nc.Block())

        def unit_source(kind, i, li):
            one = bass.ds(li, 1)
            cut = lambda ap: ap.rearrange("l (k p) n -> p (l k) n", p=P)
            if kind == "mod":
                return cut(a["w_mod"][one, :, i * 256:(i + 1) * 256]), 8, 256
            if kind == "in":
                (c0, n), half = G_COLS[i[0]], i[1]
                return cut(a["w_in"][one, half * 512:(half + 1) * 512, c0:c0 + n]), 4, n
            if kind == "uq":
                return cut(a["w_mla_uq"][one]), 2, 384
            if kind == "ukv":
                return cut(a["w_mla_ukv"][one]), 1, 512
            if kind == "gate":
                c0 = i[1] * D + i[0] * 256
                return cut(a["w_gate"][one, :, c0:c0 + 256]), 8, 256
            if kind == "out":
                return cut(a["w_out"][one, :, i * 256:(i + 1) * 256]), 8, 256
            if kind == "up":
                src = a["w_up"][one].rearrange("l (k p) (s f) -> p (l k) s f", p=P, s=2)
                return src[:, :, :, i * P:(i + 1) * P], 8, 256
            j0, nj = UP_GROUPS[i[0]]
            return cut(a["w_down"][one, j0 * P:(j0 + nj) * P, i[1] * 256:(i[1] + 1) * 256]), nj, 256

        def unit_cols(u):
            _, k, n = unit_shape[u]
            return k * n

        unit_shape = [(kind,) + {"mod": (8, 256), "uq": (2, 384), "ukv": (1, 512), "gate": (8, 256),
                                 "out": (8, 256), "up": (8, 256), "in": (4, G_COLS[i[0]][1] if kind == "in" else 0),
                                 "down": (UP_GROUPS[i[0]][1] if kind == "down" else 0, 256)}[kind]
                      for kind, i, _ in UNITS]
        SPLITS = [u for u, unit in enumerate(UNITS) if unit[2]]
        V_LOW = tuple(range(8))

        def low_ready(s):
            if s in V_LOW:
                return v_lo_done, V_LOW.index(s) + 1
            return lo_done, s + 1 - sum(v < s for v in V_LOW)


        def raw_released(u):
            kind, i, split = UNITS[u]
            if split:
                return low_ready(SPLITS.index(u))
            return {"uq": (mla_mm, 4 + T), "ukv": (mla_mm, 4 + T + 4 + T + 1)}[kind]

        def parts_released(s):
            kind, i, _ = UNITS[SPLITS[s]]
            if kind == "mod":
                return mod_mm, i + 1
            if kind == "in":
                return (z_mm, T * (i[0] + 1)) if i[1] else (half_mm, i[0] + 1)
            if kind == "gate":
                return gatew_mm, NB * i[0] + i[1] + 1
            if kind == "down":
                return down_mm, 8 * i[0] + 2 * i[1] + 2
            return (out_mm, 2 * i + 2) if kind == "out" else (up_mm, i + 1)

        @block.sync
        def _(sp):
            sp.dma_start(const[:], a["const"]).then_inc(start_loaded.sem, 16)
            sp.dma_start(crow[0:8, :], a["c_ctx"].rearrange("(k p) -> k p", p=P)).then_inc(start_loaded.sem, 16)
            sp.dma_start(crow[8:16, :], a["c"].rearrange("b (k p) -> (b k) p", p=P)).then_inc(start_loaded.sem, 16)
            sp.dma_start(x_tm[:, 0:1, :], a["x_prompt"].rearrange("b p d -> p b d")).then_inc(start_loaded.sem, 16)
            sp.dma_start(x_tm[:, 1:T, :], a["x_sample"].rearrange("b (t p) d -> p (b t) d", p=P)).then_inc(start_loaded.sem, 16)
            with sp.Fori(0, DEPTH) as li:
                now = counts(li)
                one = bass.ds(li, 1)
                loads = [0]

                def load(dst, src):
                    loads[0] += 1
                    sp.dma_start(dst, src).then_inc(small.sem, 16)

                sp.wait_ge(raw_free.sem, now(raw_free, 1))
                vec = lambda n: a[n][one].rearrange("l (k p) -> (l k) p", p=P)
                load(rows[0:48, 0, :], vec("b_mod"))
                load(rows[48:56, 0, :], vec("g_mix"))
                load(rows[56:64, 0, :], vec("g_ffn"))
                load(rows[64:96, 0, :], vec("b_gate"))
                load(rows[0:44, 1, :], vec("b_up"))
                load(rows[44:88, 1, :], vec("b_conv"))
                taps = lambda w: a["w_conv"][one, w:w + 1].rearrange("l w (k p) -> (l w k) p", p=P)
                load(rows[0:44, 2, :], taps(0))
                load(rows[44:88, 2, :], taps(1))
                load(rows[0:44, 3, :], taps(2))
                load(decay[:, 0:8], a["ret_decay"][one].rearrange("l r h -> l (r h)").to_broadcast([P, 8]))
                load(sink[:], a["win_sink"][one].to_broadcast([P, 4]))
                load(dlam[:].rearrange("p a b -> p (a b)"), a["diff_lambda"][one].rearrange("l a b -> l (a b)").to_broadcast([P, 128]))
                load(g_diff[:], a["g_diff"][one].to_broadcast([P, 64]))
                load(g_mq[:], a["g_mla_q"][one].to_broadcast([P, BW]))
                load(g_mkv[:], a["g_mla_kv"][one].to_broadcast([P, P]))
                for name, lo, n in (("cache_win_k", 0, 128), ("cache_win_v", 128, 128), ("cache_diff_k", 256, 256),
                                    ("cache_diff_v", 512, 256)):
                    load(cache[:, lo:lo + n], a[name][0, one].rearrange("l p h d -> p (l h d)"))
                load(cache[:, 768:896], a["cache_mla_ckv"][0, one].rearrange("l p d -> p (l d)"))
                load(cache[:, 896:928], a["cache_mla_krope"][0, one].rearrange("l p d -> p (l d)"))
                for r in range(2):
                    for j in range(2):
                        load(state0[:, r, j, :], a["state_ret"][0, one, r, 2 * j:2 * j + 2].rearrange("l e d v -> (l e d) v"))
                assert loads[0] == N_SMALL, loads
                for u, (kind, i, _) in enumerate(UNITS):
                    src, k, n = unit_source(kind, i, li)
                    dst = raw[u % RAW][:, 0:k * n].rearrange("p (k n) -> p k n", k=k)
                    if u >= RAW:
                        sig, count = raw_released(u - RAW)
                        sp.wait_ge(sig.sem, now(sig, count))
                    for part in range(unit_loads(u)):
                        if kind == "up":
                            sp.dma_start(dst[:, :, part * P:(part + 1) * P], src[:, :, part]).then_inc(raw_loaded[u % RAW].sem, 16)
                        else:
                            sp.dma_start(dst, src).then_inc(raw_loaded[u % RAW].sem, 16)
            sp.wait_ge(x_down.sem, DEPTH * x_down.per)
            sp.dma_start(g_fin[:], a["g_final"].unsqueeze(0).to_broadcast([P, D])).then_inc(gfin.sem, 16)
            for t in range(T):
                sp.wait_ge(y_done.sem, t + 1)
                dst = y_prompt.rearrange("b p d -> p b d") if t == 0 else y_sample[:, (t - 1) * P:t * P, :].rearrange("b p d -> p b d")
                sp.dma_start(dst, y_tm[:, t:t + 1, :]).then_inc(y_out.sem, 16)
            sp.wait_ge(y_out.sem, 16 * T)

        @block.gpsimd
        def _(pool):
            pool.memset(token[:], 0.0).then_inc(raw_free.sem, 1)
            with pool.Fori(0, DEPTH) as li:
                now = counts(li)
                for s, u in enumerate(SPLITS):
                    if s in V_LOW:
                        continue
                    n = unit_cols(u)
                    pool.wait_ge(hi_done.sem, now(hi_done, s + 1))
                    nc.gpsimd.tensor_tensor(w_lo[s % WS][:, 0:n], raw[u % RAW][:, 0:n], w_hi[s % WS][:, 0:n].bitcast(F32),
                                            ALU.subtract).then_inc(lo_done.sem, 1)
                pool.memset(token[:], 0.0).then_inc(raw_free.sem, 1)

        @block.tensor
        def _(pe):
            mm, tr = nc.tensor.matmul, nc.tensor.transpose
            pe.wait_ge(start_loaded.sem, 80)
            tr(bank(7, 0, 16), crow[:, :], ident[0:16, 0:16]).then_inc(cond_t.sem, 1)
            for k in range(KD):
                b = 2 * (k % 3)
                if k >= 3:
                    pe.wait_ge(xin_done.sem, k - 2)
                for t in range(T):
                    last = tr(bank(b, t * P, t * P + P), x_tm[:, t, k * P:(k + 1) * P], ident)
                last.then_inc(xin_t.sem, 1)
            pe.wait_ge(xin_done.sem, KD)
            pe.wait_ge(cond_done.sem, 3)
            pe.wait_ge(made.sem, 3)

            with pe.Fori(0, DEPTH) as li:
                now = counts(li)
                nxt = {"u": 0, "s": 0}

                def raw_unit(kind):
                    u = nxt["u"]
                    assert UNITS[u][0] == kind and not UNITS[u][2], (kind, UNITS[u])
                    nxt["u"] += 1
                    pe.wait_ge(raw_loaded[u % RAW].sem, now(raw_loaded[u % RAW], loaded_count(u)))
                    _, k, n = unit_shape[u]
                    return raw[u % RAW][:, 0:k * n].rearrange("p (k n) -> p k n", k=k)

                def split_unit(kind):
                    u, s = nxt["u"], nxt["s"]
                    assert UNITS[u][0] == kind and UNITS[u][2], (kind, UNITS[u])
                    nxt["u"], nxt["s"] = u + 1, s + 1
                    sig, count = low_ready(s)
                    pe.wait_ge(sig.sem, now(sig, count))
                    _, k, n = unit_shape[u]
                    return [w[s % WS][:, 0:k * n].rearrange("p (k n) -> p k n", k=k) for w in (w_hi, w_lo)]

                def product3(outs2, w_hl, w_at, x_hl, x_at, first, final):
                    for q, (wi, xi) in enumerate(((0, 0), (0, 1), (1, 0))):
                        for out, at_ in zip(outs2, x_at):
                            ins = mm(out, w_at(w_hl[wi]), at_(x_hl[xi]), start=first and q == 0, stop=final and q == 2)
                    return ins

                def mod_unit(i):
                    w_hl = split_unit("mod")
                    if i >= 2:
                        pe.wait_ge(row_done.sem, now(row_done, i - 1 if i < 8 else i))
                    c0 = mod_col(i)
                    for k in range(KD):
                        for q in range(2):
                            last = mm(ps[0:4, c0:c0 + 256], cond_r[:, k, :], w_hl[q][:, k, :],
                                      start=k == 0 and q == 0, stop=k == KD - 1 and q == 1)
                    last.then_inc(mod_mm.sem, 1)

                def mod_transpose(i):
                    pe.wait_ge(row_done.sem, now(row_done, i + 1))
                    if i:
                        pe.wait_ge(mod_done.sem, now(mod_done, i))
                    for m in range(2):
                        c0 = mod_t_col(i) + 2 * m
                        last = mm(ps[:, c0:c0 + 2], mod_row[0:4, i % 2, m * P:(m + 1) * P], c("fold")[0:4, :], start=True, stop=True)
                    last.then_inc(mod_t.sem, 1)

                def token_sums(i):
                    pe.wait_ge(ss_done[i].sem, now(ss_done[i], 1))
                    for t in range(T):
                        last = mm(bank(4, t, t + 1), ss[:, t * P:(t + 1) * P], ones[:, 0:1], start=True, stop=True)
                    last.then_inc(ss_mm.sem, 1)

                def spread_rstd(i):
                    pe.wait_ge(diag_done.sem, now(diag_done, i + 1))
                    for t in range(T):
                        last = mm(bank(6, t * P, t * P + P), ones[:], diag[:, t, :], start=True, stop=True)
                    last.then_inc(bc_mm.sem, 1)

                def in_product(g):
                    n, base = G_COLS[g][1], 5 if g in (1, 4) else 0
                    for half in range(2):
                        w_hl = split_unit("in")
                        steps = [(k4, t) for k4 in range(4) for t in range(T)] if half == 0 else \
                            [(k4, t) for t in range(T) for k4 in range(4)]
                        for k4, t in steps:
                            k = 4 * half + k4
                            if g == 0 and t == 0:
                                pe.wait_ge(h_done.sem, now(h_done, k + 1))
                            b = (base + t) % 8
                            if k == 0 and g in (1, 4) and b < 2:
                                pe.wait_ge(z_done.sem, now(z_done, T * (g - 1) + b + 1))
                            for q, (xi, wi) in enumerate(((0, 0), (0, 1), (1, 0))):
                                last = mm(bank(b, 0, n), (h_hi, h_lo)[xi][:, k, t * P:(t + 1) * P], w_hl[wi][:, k4, :],
                                          start=k == 0 and q == 0, stop=k == KD - 1 and q == 2)
                            if k == KD - 1:
                                last.then_inc(z_mm.sem, 1)
                        if half == 0:
                            last.then_inc(half_mm.sem, 1)

                def o_transposes(br):
                    for c2 in range(2):
                        for t in range(T):
                            last = tr(bank(2 * c2, t * P, t * P + P), o_tm[:, t, c2 * P:(c2 + 1) * P], ident)
                        last.then_inc(ot_mm.sem, 1)

                def attention(br):
                    head0 = 4 * T * (br - 1)
                    for i in range(STEPS):
                        if i < 4 * T:
                            a_ = head0 + i
                            _, t, h = HEADS[a_]
                            for m2 in range(2 if br == 2 else 1):
                                m = FIRST_MAP[a_] + m2
                                if m >= 2:
                                    pe.wait_ge(exp_done.sem, now(exp_done, m - 1))
                                b = 2 * (m % 2)
                                for col, k0, n in score_runs(key_blocks(br, t)):
                                    last = mm(bank(b, col, col + n), query(br, t, h, m2), keys(br, h, m2, k0, n),
                                              start=True, stop=True)
                                last.then_inc(s_mm.sem, 1)
                        if 1 <= i <= 4 * T:
                            a_ = head0 + i - 1
                            m = FIRST_MAP[a_]
                            if br == 2:
                                pe.wait_ge(comb_done.sem, now(comb_done, i))
                            else:
                                pe.wait_ge(exp_done.sem, now(exp_done, m + 1))
                            if br == 1 and a_ >= 2:
                                pe.wait_ge(pt_done.sem, now(pt_done, a_ - 1))
                            if br > 1:
                                pe.wait_ge(pt_done.sem, now(pt_done, a_))
                            for j in range(len(key_blocks(br, HEADS[a_][1]))):
                                last = tr(bank(pt_bank(br, a_), j * P, j * P + P), probs[:, m % 4, j * P:(j + 1) * P], ident)
                            last.then_inc(pt_mm.sem, 1)
                        if 2 <= i <= 4 * T + 1:
                            a_ = head0 + i - 2
                            _, t, h = HEADS[a_]
                            pe.wait_ge(pt_done.sem, now(pt_done, a_ + 1))
                            if h == 0 and a_:
                                pe.wait_ge(oev_done.sem, now(oev_done, T * (br - 1) + t))
                            if i - 1 in MOD_STEPS[br] and (br > 1 or i - 1 != MOD_STEPS[br][0]):
                                n_mod = 8 + 5 * (br - 1) + MOD_STEPS[br].index(i - 1)
                                pe.wait_ge(mod_done.sem, now(mod_done, n_mod))
                            kb = key_blocks(br, t)
                            for j, b in enumerate(kb):
                                last = mm(bank(6, 64 * h, 64 * h + 64), probs_t[:, a_ % 2, j, :], values(br, b, h),
                                          start=j == 0, stop=j == len(kb) - 1)
                            last.then_inc(pv_mm.sem, 1)
                        if i in MOD_STEPS[br]:
                            n_mod = 8 + 5 * (br - 1) + MOD_STEPS[br].index(i)
                            mod_unit(n_mod)
                            if n_mod > 8:
                                mod_transpose(n_mod - 1)

                pe.wait_ge(small.sem, now(small, 16 * N_SMALL))
                for s, (n, c0) in enumerate(((96, 0), (88, 96), (88, 184), (44, 272))):
                    last = tr(bank(0, c0, c0 + n), rows[0:n, s, :], ident[0:n, 0:n])
                last.then_inc(vec_t.sem, 1)
                token_sums(0)
                for i in range(8):
                    mod_unit(i)
                    if i:
                        mod_transpose(i - 1)
                    if i == 2:
                        spread_rstd(0)
                mod_transpose(7)
                pe.wait_ge(vec_done.sem, now(vec_done, 1))
                in_product(0)
                in_product(1)

                for t in range(T):
                    pe.wait_ge(z_done.sem, now(z_done, t + 1))
                    if t >= 2:
                        pe.wait_ge(rt_done.sem, now(rt_done, t - 1))
                    else:
                        pe.wait_ge(z_done.sem, now(z_done, t + 3))
                    for j in range(4):
                        last = tr(bank(2 + t % 2, j * P, j * P + P), z[0][:, t, j * P:(j + 1) * P], ident)
                    last.then_inc(rt_mm.sem, 1)
                for t in range(T):
                    pe.wait_ge(kd_done.sem, now(kd_done, t + 1))
                    pe.wait_ge(z_done.sem, now(z_done, T + t + 1))
                    for r in range(2):
                        for h in range(4):
                            p0, c0 = 64 * (h % 2), 256 * (t % 2) + 128 * r + 64 * (h // 2)
                            last = mm(ps[p0:p0 + 64, (4 + t // 2) * BANK + c0:(4 + t // 2) * BANK + c0 + 64], kd[:, t % 2, 4 * r + h, :],
                                      z[1][:, t, 64 * h:64 * h + 64], start=True, stop=True)
                    last.then_inc(u_mm.sem, 1)
                for i in range(T + 1):
                    if i < T:
                        t = i
                        pe.wait_ge(rt_done.sem, now(rt_done, T))
                        if t >= 2:
                            pe.wait_ge(rst_done.sem, now(rst_done, 2 * t - 2))
                        for odd in range(2):
                            for j in range(2):
                                last = mm(bank(2 * (t % 2) + odd, j * P, j * P + P), rqk[64 * odd:64 * odd + 64, 2 + j, t * P:(t + 1) * P],
                                          rqk[64 * odd:64 * odd + 64, j, t * P:(t + 1) * P], start=True, stop=True)
                        last.then_inc(rs_mm.sem, 1)
                    if i:
                        t = i - 1
                        pe.wait_ge(rst_done.sem, now(rst_done, 2 * t + 2))
                        pe.wait_ge(s_done.sem, now(s_done, 1))
                        if t >= 2:
                            pe.wait_ge(ro_done.sem, now(ro_done, t - 1))
                        b = 6 if t % 2 == 0 else 4
                        for odd in range(2):
                            for j in range(2):
                                h = 2 * j + odd
                                out = bank(b + odd, 64 * j, 64 * j + 64)
                                last = mm(out, st_dec[:, t % 2, 2 * odd + j, :], z[1][:, t, 64 * h:64 * h + 64], start=True, stop=t == 0)
                                for r in range(2 if t else 0):
                                    s_at = state_of(r, t - 1)
                                    last = mm(out, q_dec[64 * odd:64 * odd + 64, t % 2, 2 * r + j, :], s_at[64 * odd:64 * odd + 64, j, :],
                                              start=False, stop=r == 1)
                        last.then_inc(ro_mm.sem, 1)

                pe.wait_ge(ro_done.sem, now(ro_done, T))
                in_product(2)
                pe.wait_ge(z_done.sem, now(z_done, 3 * T))
                pe.wait_ge(ret_o.sem, now(ret_o, 1))
                o_transposes(0)
                pe.wait_ge(rope_done.sem, now(rope_done, 1))
                for r in range(3):
                    if r == 2:
                        pe.wait_ge(ot_done.sem, now(ot_done, 1))
                    b = (4, 6, 0)[r]
                    for t in range(T + (r == 2)):
                        if r == 2:
                            src = z[0][:, t, 256:384] if t < T else cache[:, 0:128]
                        else:
                            src = z[0][:, t, r * P:(r + 1) * P]
                        last = tr(bank(b, t * P, t * P + P), src, ident)
                    last.then_inc(qk_mm.sem, 1)
                pe.wait_ge(qk_done.sem, now(qk_done, 3))
                pe.wait_ge(ot_done.sem, now(ot_done, 2))
                attention(1)

                pe.wait_ge(pt_done.sem, now(pt_done, 4 * T))
                in_product(3)
                pe.wait_ge(oev_done.sem, now(oev_done, T))
                pe.wait_ge(row_done.sem, now(row_done, 13))
                pe.wait_ge(mod_done.sem, now(mod_done, 12))
                in_product(4)
                pe.wait_ge(z_done.sem, now(z_done, 5 * T))
                o_transposes(1)
                pe.wait_ge(rope_done.sem, now(rope_done, 2))
                for r in range(4):
                    if r >= 2:
                        pe.wait_ge(ot_done.sem, now(ot_done, 2 + r - 1))
                    b = (4, 6, 0, 2)[r]
                    for t in range(T + (r >= 2)):
                        src = z[0][:, t, r * P:(r + 1) * P] if t < T else cache[:, 256 + (r - 2) * P:256 + (r - 1) * P]
                        last = tr(bank(b, t * P, t * P + P), src, ident)
                    last.then_inc(qk_mm.sem, 1)
                pe.wait_ge(qk_done.sem, now(qk_done, 7))
                attention(2)

                in_product(5)
                pe.wait_ge(z_done.sem, now(z_done, 6 * T))
                pe.wait_ge(diff_o.sem, now(diff_o, 1))
                o_transposes(2)
                pe.wait_ge(prep_done.sem, now(prep_done, 1))
                pe.wait_ge(pt_done.sem, now(pt_done, 8 * T))
                pe.wait_ge(oev_done.sem, now(oev_done, 2 * T))
                pe.wait_ge(row_done.sem, now(row_done, 18))
                pe.wait_ge(mod_done.sem, now(mod_done, 17))
                n_item = [0]

                def slot():
                    k = n_item[0]
                    n_item[0] += 1
                    if k in (2, 3):
                        pe.wait_ge(ot_done.sem, now(ot_done, 4 + k - 1))
                    if k >= 4:
                        pe.wait_ge(mla_done.sem, now(mla_done, k - 3))
                    return 2 * ((k + 2) % 4)

                for r in range(2):
                    b = slot()
                    for t in range(T):
                        last = tr(bank(b, t * P, t * P + P), z[1][:, t, 256 + r * P:256 + (r + 1) * P], ident)
                    last.then_inc(mla_mm.sem, 1)
                b = slot()
                for t in range(T + 1):
                    last = tr(bank(b, t * P, t * P + P), z5[:, t, 0:128] if t < T else cache[:, 768:896], ident)
                last.then_inc(mla_mm.sem, 1)
                b = slot()
                for t in range(T + 1):
                    last = tr(ps[0:32, b * BANK + t * P:b * BANK + t * P + P], z5[:, t, 128:160] if t < T else cache[:, 896:928], ident)
                last.then_inc(mla_mm.sem, 1)
                w = raw_unit("uq")
                for t in range(T):
                    b = slot()
                    pe.wait_ge(mla_done.sem, now(mla_done, 2))
                    for k in range(2):
                        last = mm(bank(b, 0, 384), cq_t[:, k, t * P:(t + 1) * P], w[:, k, :], start=k == 0, stop=k == 1)
                    last.then_inc(mla_mm.sem, 1)
                w = raw_unit("ukv")
                pe.wait_ge(mla_done.sem, now(mla_done, 3))
                for h in range(4):
                    b = slot()
                    for c0, n in ((0, 512), (512, 256)):
                        last = mm(ps[0:64, b * BANK + c0:b * BANK + c0 + n], w[:, 0, P * h:P * h + 64], ckv_t[:, c0:c0 + n],
                                  start=True, stop=True)
                    last.then_inc(mla_mm.sem, 1)
                for t in range(T + 1):
                    b = slot()
                    last = mm(bank(b, 0, 256), ckv_t[:, t * P:(t + 1) * P], w[:, 0, :].rearrange("p (h s d) -> p s h d", h=4, s=2)[:, 1],
                              start=True, stop=True)
                    last.then_inc(mla_mm.sem, 1)
                pe.wait_ge(rope_done.sem, now(rope_done, 3))
                for h in range(4):
                    b = slot()
                    for t in range(T):
                        last = tr(ps[0:96, b * BANK + t * P:b * BANK + t * P + P], z_mq[:, t, 96 * h:96 * h + 96], ident)
                    last.then_inc(mla_mm.sem, 1)
                pe.wait_ge(mla_done.sem, now(mla_done, MLA_ITEMS))
                attention(3)
                pe.wait_ge(oev_done.sem, now(oev_done, 3 * T))
                mod_transpose(23)

                halves = [lambda ap, q=q: ap[:, q * HALF:(q + 1) * HALF] for q in range(2)]
                for mp in range(4):
                    wb = w_br[mp % 2]
                    for n in range(NB):
                        w_hl = split_unit("gate")
                        for m in range(2):
                            i = 8 * mp + 2 * n + m
                            s4 = 4 * (i % 2)
                            if i >= 2:
                                pe.wait_ge(gate_read.sem, now(gate_read, i - 1))
                            if i < 2:
                                pe.wait_ge(exp_done.sem, now(exp_done, N_MAPS))
                                pe.wait_ge(pt_done.sem, now(pt_done, N_HEADS))
                                pe.wait_ge(oev_done.sem, now(oev_done, 3 * T))
                                pe.wait_ge(mod_done.sem, now(mod_done, 24))
                            if i == 6:
                                o_transposes(3)
                                pe.wait_ge(ot_done.sem, now(ot_done, 8))
                            for k in range(KD):
                                last = product3([bank(s4, 0, HALF), bank(s4 + 1, 0, HALF)], w_hl,
                                                lambda w: w[:, k, m * P:(m + 1) * P],
                                                (h_hi[:, k], h_lo[:, k]), halves, k == 0, k == KD - 1)
                            if m:
                                last.then_inc(gatew_mm.sem, 1)
                            if n == 0 and m == 0:
                                pe.wait_ge(branch_loaded[mp % 2].sem, now(branch_loaded[mp % 2], 16 * (mp // 2 + 1)))
                            for k in range(2):
                                for q in range(2):
                                    last = mm(bank(s4 + 2 + q, 0, HALF), wb[:, 2 * n + k, m * P:(m + 1) * P],
                                              o_t[:, 2 * n + k, q * HALF:(q + 1) * HALF], start=k == 0, stop=k == 1)
                            last.then_inc(gate_mm.sem, 1)

                pe.wait_ge(gate_read.sem, now(gate_read, 32))
                for mp in range(4):
                    w_hl = split_unit("out")
                    for m2 in range(2):
                        m = 2 * mp + m2
                        b = 2 * (m % 2)
                        if m >= 2:
                            pe.wait_ge(x_out.sem, now(x_out, m - 1))
                        for k in range(KD):
                            if m == 0:
                                pe.wait_ge(mix_done.sem, now(mix_done, k + 1))
                            last = product3([bank(b, 0, HALF), bank(b + 1, 0, HALF)], w_hl, lambda w: w[:, k, m2 * P:(m2 + 1) * P],
                                            (mix_hi[:, k], mix_lo[:, k]), halves, k == 0, k == KD - 1)
                        last.then_inc(out_mm.sem, 1)
                token_sums(1)
                spread_rstd(1)

                wide = [lambda ap: ap[:, 0:322], lambda ap: ap[:, 322:PADDED]]
                for g, (j0, nj) in enumerate(UP_GROUPS):
                    for j in range(j0, j0 + nj):
                        w_hl = split_unit("up")
                        s4 = 4 * (j % 2)
                        if j >= 2:
                            pe.wait_ge(up_done.sem, now(up_done, j - 1))
                        if j in (j0, j0 + 1):
                            pe.wait_ge(x_out.sem, now(x_out, 8)) if g == 0 else pe.wait_ge(x_down.sem, now(x_down, 8 * g))
                        if j == 1:
                            pe.wait_ge(h_done.sem, now(h_done, 16))
                        for k in range(KD):
                            if j == 0:
                                pe.wait_ge(h_done.sem, now(h_done, 8 + k + 1))
                            for part in range(2):
                                last = product3([bank(s4 + 2 * part, 0, HALF), bank(s4 + 2 * part + 1, 0, HALF)], w_hl,
                                                lambda w: w[:, k, part * P:(part + 1) * P], (h_hi[:, k], h_lo[:, k]), halves,
                                                k == 0, k == KD - 1)
                        last.then_inc(up_mm.sem, 1)
                    pe.wait_ge(up_done.sem, now(up_done, j0 + nj))
                    for mp in range(4):
                        w_hl = split_unit("down")
                        for m2 in range(2):
                            m = 8 * g + 2 * mp + m2
                            b = 2 * (m % 2)
                            if m % 8 >= 2:
                                pe.wait_ge(x_down.sem, now(x_down, m - 1))
                            for k in range(nj):
                                if mp == 0 and m2 == 0:
                                    pe.wait_ge(al_done.sem, now(al_done, j0 + k + 1))
                                sl = (j0 + k) % ACT_SLOTS
                                last = product3([bank(b, 0, 322), bank(b + 1, 0, 320)], w_hl, lambda w: w[:, k, m2 * P:(m2 + 1) * P],
                                                (a_hi[:, sl], a_lo[:, sl]), wide, k == 0, k == nj - 1)
                            last.then_inc(down_mm.sem, 1)
                assert nxt == {"u": N_UNITS, "s": N_SPLIT}
                pe.wait_ge(x_down.sem, now(x_down, 24))
            pe.wait_ge(ss_done[0].sem, DEPTH + 1)
            for t in range(T):
                last = mm(bank(4, t, t + 1), ss[:, t * P:(t + 1) * P], ones[:, 0:1], start=True, stop=True)
            last.then_inc(yss_mm.sem, 1)
            pe.wait_ge(yst_done.sem, 1)
            for t in range(T):
                if t == 4:
                    pe.wait_ge(y_done.sem, 1)
                for k in range(KD):
                    last = tr(bank(2 * (t % 4), k * P, k * P + P), x[:, k, t * P:(t + 1) * P], ident)
                last.then_inc(yt_mm.sem, 1)

        @block.scalar
        def _(sc):
            act_ = nc.scalar.activation
            sc.wait_ge(cond_raw.sem, 1)
            act_(stat[:, 0:2, :].rearrange("p a b -> p (a b)"), cond[:], ACT.Sigmoid).then_inc(cond_sig.sem, 1)
            for k in range(KD):
                sc.wait_ge(xin_t.sem, k + 1)
                act_(x[:, k, :], bank(2 * (k % 3), 0, TOK), ACT.Copy).then_inc(xin_done.sem, 1)
            with sc.Fori(0, DEPTH) as li:
                now = counts(li)
                one = bass.ds(li, 1)
                nxt = [0]

                def round_unit():
                    s = nxt[0]
                    nxt[0] += 1
                    u = SPLITS[s]
                    n = unit_cols(u)
                    sc.wait_ge(raw_loaded[u % RAW].sem, now(raw_loaded[u % RAW], loaded_count(u)))
                    if s >= WS:
                        sig, count = parts_released(s - WS)
                        sc.wait_ge(sig.sem, now(sig, count))
                    act_(w_hi[s % WS][:, 0:n], raw[u % RAW][:, 0:n], ACT.Copy).then_inc(hi_done.sem, 1)

                def take_row(i):
                    sc.wait_ge(mod_mm.sem, now(mod_mm, i + 1))
                    if i >= 2:
                        sc.wait_ge(mod_t.sem, now(mod_t, i - 1))
                    act_(mod_row[0:4, i % 2, :], ps[0:4, mod_col(i):mod_col(i) + 256], ACT.Copy).then_inc(row_done.sem, 1)

                def norm(i):
                    if i == 0:
                        round_unit()
                        round_unit()
                    sc.wait_ge(ss_mm.sem, now(ss_mm, i + 1))
                    act_(st5[:, 0, 0:T], bank(4, 0, T), ACT.Sqrt, bias=eps_c[:], scale=1.0 / D).then_inc(rms_done.sem, 1)
                    if i == 0:
                        for n in range(8):
                            take_row(n)
                            round_unit()
                    else:
                        round_unit()
                    sc.wait_ge(scl_done.sem, now(scl_done, i + 1))
                    for k in range(KD):
                        sc.wait_ge(t1_done.sem, now(t1_done, 8 * i + k + 1))
                        if k >= 2:
                            sc.wait_ge(h_done.sem, now(h_done, 8 * i + k - 1))
                        for w, (c0, c1) in enumerate(((0, CTX), (CTX, TOK))):
                            ins = act_(hf[:, k % 2, c0:c1], t1[:, k % 2, c0:c1], ACT.Identity, bias=mod[:, 24 * i + k, w:w + 1],
                                       scale=scl[:, i, k, w:w + 1])
                        ins.then_inc(hf_done.sem, 1)
                        sc.wait_ge(hf_done.sem, now(hf_done, 8 * i + k + 1))
                        act_(h_hi[:, k, :], hf[:, k % 2, :], ACT.Copy).then_inc(hh_done.sem, 1)

                def take_z(g):
                    n, b0 = G_COLS[g][1], 5 if g in (1, 4) else 0
                    for t in range(T):
                        sc.wait_ge(z_mm.sem, now(z_mm, T * g + t + 1))
                        dst = z5[:, t, :] if g == 5 else z[{1: 1, 4: 1}.get(g, 0)][:, t, :]
                        act_(dst, bank((b0 + t) % 8, 0, n), ACT.Copy).then_inc(z_done.sem, 1)

                def store(dst, src):
                    sc.dma_start(dst, src).then_inc(cache_out.sem, 16)

                def take_o(br):
                    for c2 in range(2):
                        sc.wait_ge(ot_mm.sem, now(ot_mm, 2 * br + c2 + 1))
                        act_(o_t[:, 2 * br + c2, :], bank(2 * c2, 0, TOK), ACT.Copy).then_inc(ot_done.sem, 1)

                def attention(br):
                    head0 = 4 * T * (br - 1)
                    for i in range(STEPS):
                        if i < 4 * T:
                            a_ = head0 + i
                            _, t, h = HEADS[a_]
                            nk = P * len(key_blocks(br, t))
                            for m2 in range(2 if br == 2 else 1):
                                m = FIRST_MAP[a_] + m2
                                sc.wait_ge(bias_done.sem, now(bias_done, m + 1))
                                if m >= 4:
                                    sc.wait_ge(pt_mm.sem, now(pt_mm, MAPS[m - 4][0] + 1))
                                bias = stat[:, 1, m % 8:m % 8 + 1]
                                if br == 1:
                                    act_(stat[:, 3, m % 8:m % 8 + 1], sink[:, h:h + 1], ACT.Exp, bias=bias)
                                act_(probs[:, m % 4, 0:nk], bank(2 * (m % 2), 0, nk), ACT.Exp, bias=bias, scale=SCALES[br],
                                     accum_out=stat[:, 2, m % 8:m % 8 + 1]).then_inc(exp_done.sem, 1)
                        if 1 <= i <= 4 * T:
                            a_ = head0 + i - 1
                            nk = P * len(key_blocks(br, HEADS[a_][1]))
                            sc.wait_ge(pt_mm.sem, now(pt_mm, a_ + 1))
                            if a_ >= 2:
                                sc.wait_ge(pv_mm.sem, now(pv_mm, a_ - 1))
                            act_(probs_t[:, a_ % 2].rearrange("p b q -> p (b q)")[:, 0:nk], bank(pt_bank(br, a_), 0, nk), ACT.Copy)\
                                .then_inc(pt_done.sem, 1)
                        if i in MOD_STEPS[br]:
                            take_row(8 + 5 * (br - 1) + MOD_STEPS[br].index(i))
                            round_unit()

                norm(0)
                sc.wait_ge(tab_arg.sem, now(tab_arg, 1))
                act_(dec_t[:, 1, :], dec_t[:, 0, :], ACT.Exp, scale=-1.0)
                act_(dsum[:, 2:4], dsum[:, 0:2], ACT.Exp).then_inc(tab_exp.sem, 1)
                round_unit()
                take_z(0)
                round_unit()
                sc.wait_ge(tab_arg.sem, now(tab_arg, 2))
                for odd in range(2):
                    for j in range(2):
                        h = 2 * j + odd
                        act_(decay_f[:, 2 * odd + j, :], c("dpos"), ACT.Exp, scale=lgam[:, h:h + 1])
                        act_(decay_b[:, 2 * odd + j, :], c("dneg"), ACT.Exp, scale=lgam[:, 4 + h:5 + h])
                for r in range(2):
                    for j in range(2):
                        act_(qdec[:, 2 * r + j, :], c("rowb" if r else "rowf"), ACT.Exp, scale=lgam[:, 8 + 2 * r + j:9 + 2 * r + j])
                    act_(kdec[:, r, :], lgam[:, 4 * r:4 * r + 4], ACT.Exp, scale=c("colb" if r else "colf"))
                act_(cdec[:], lgam[:, 8:12], ACT.Exp, scale=float(P)).then_inc(tab_exp.sem, 1)
                round_unit()
                take_z(1)
                round_unit()

                for t in range(T):
                    sc.wait_ge(rt_mm.sem, now(rt_mm, t + 1))
                    act_(rqk[:, :, t * P:(t + 1) * P], bank(2 + t % 2).rearrange("p (j n) -> p j n", j=4), ACT.Copy)\
                        .then_inc(rt_done.sem, 1)
                sc.wait_ge(st_out.sem, now(st_out, 1))
                for r in range(2):
                    for j in range(2):
                        store(o_state[0, one, r, 2 * j:2 * j + 2].rearrange("l e d v -> (l e d) v"), state_c[:, 2 * r + j, :])
                for t in range(T):
                    sc.wait_ge(ro_mm.sem, now(ro_mm, t + 1))
                    b = 6 if t % 2 == 0 else 4
                    src = ps[:, b * BANK:(b + 2) * BANK].rearrange("p (e n) -> p e n", e=2)[:, :, 0:128].rearrange("p e (j d) -> p e j d", j=2)
                    act_(o_tm[:, t, :].rearrange("p (j e d) -> p e j d", j=2, e=2), src, ACT.Copy).then_inc(ro_done.sem, 1)
                sc.wait_ge(post_in.sem, now(post_in, 1))
                act_(o_tm[:], post[:], ACT.Square).then_inc(post_act.sem, 1)
                sc.wait_ge(post_in.sem, now(post_in, 2))
                act_(st5[:, 3, :], st5[:, 2, :], ACT.Sqrt, bias=eps_c[:], scale=1.0 / 64).then_inc(post_act.sem, 1)
                act_(o_tm[:], z[1][:, :, 256:512], ACT.Sigmoid).then_inc(post_act.sem, 1)
                take_z(2)
                sc.wait_ge(z_done.sem, now(z_done, 3 * T))
                store(o_win_k[0, one].rearrange("l p h d -> p (l h d)"), z[0][:, 0, 256:384])
                store(o_win_v[0, one].rearrange("l p h d -> p (l h d)"), z[0][:, 0, 384:512])
                round_unit()
                round_unit()
                take_o(0)
                for r in range(3):
                    sc.wait_ge(qk_mm.sem, now(qk_mm, r + 1))
                    if r == 2:
                        for half_ in range(2):
                            for g in range(2):
                                ins = act_(wk_t[64 * half_:64 * half_ + 64, g, :], ps[64 * g:64 * g + 64, 0:KEYS], ACT.Copy)
                        ins.then_inc(qk_done.sem, 1)
                    else:
                        act_(wq_t[:, r, :], bank(4 + 2 * r, 0, TOK), ACT.Copy).then_inc(qk_done.sem, 1)
                sc.wait_ge(cache_out.sem, now(cache_out, 16 * 6))
                attention(1)

                round_unit()
                take_z(3)
                round_unit()
                sc.wait_ge(z_done.sem, now(z_done, 4 * T))
                store(o_diff_k[0, one].rearrange("l p h d -> p (l h d)"), z[0][:, 0, 256:512])
                take_z(4)
                sc.wait_ge(z_done.sem, now(z_done, 5 * T))
                store(o_diff_v[0, one].rearrange("l p h d -> p (l h d)"), z[1][:, 0, 0:256])
                round_unit()
                round_unit()
                take_o(1)
                for r in range(4):
                    sc.wait_ge(qk_mm.sem, now(qk_mm, 3 + r + 1))
                    if r >= 2:
                        act_(dk_t[:, r - 2, :], bank((0, 2)[r - 2], 0, KEYS), ACT.Copy).then_inc(qk_done.sem, 1)
                    else:
                        act_(dq_t[:, r, :], bank(4 + 2 * r, 0, TOK), ACT.Copy).then_inc(qk_done.sem, 1)
                attention(2)

                sc.wait_ge(cache_out.sem, now(cache_out, 16 * 8))
                sc.wait_ge(post_in.sem, now(post_in, 3))
                act_(post[:], o_tm[:], ACT.Square).then_inc(post_act.sem, 1)
                sc.wait_ge(post_in.sem, now(post_in, 4))
                act_(st5[:, 3, :], st5[:, 2, :], ACT.Sqrt, bias=eps_c[:], scale=1.0 / 64).then_inc(post_act.sem, 1)
                act_(post[:], z[1][:, :, 256:512], ACT.Square).then_inc(prep_act.sem, 1)
                sc.wait_ge(prep_in.sem, now(prep_in, 1))
                act_(st5[:, 1, 0:T], st5[:, 0, 0:T], ACT.Sqrt, bias=eps_c[:], scale=1.0 / BW).then_inc(prep_act.sem, 1)
                take_z(5)
                round_unit()
                sc.wait_ge(z_done.sem, now(z_done, 6 * T))
                act_(sq_kv[:], z5[:, :, 0:128], ACT.Square).then_inc(prep_act.sem, 1)
                sc.wait_ge(prep_in.sem, now(prep_in, 2))
                act_(st5[:, 1, T:2 * T], st5[:, 0, T:2 * T], ACT.Sqrt, bias=eps_c[:], scale=1.0 / P).then_inc(prep_act.sem, 1)
                take_o(2)
                sc.wait_ge(prep_done.sem, now(prep_done, 1))
                store(o_ckv[0, one].rearrange("l p d -> p (l d)"), z5[:, 0, 0:128])
                store(o_krope[0, one].rearrange("l p d -> p (l d)"), z5[:, 0, 128:160])
                k = 0

                def take(dst, rows_, n, src=None):
                    nonlocal k
                    sc.wait_ge(mla_mm.sem, now(mla_mm, k + 1))
                    b = 2 * ((k + 2) % 4)
                    act_(dst, ps[0:rows_, b * BANK:b * BANK + n] if src is None else src(b), ACT.Copy).then_inc(mla_done.sem, 1)
                    k += 1

                for r in range(2):
                    take(cq_t[:, r, :], P, TOK)
                take(ckv_t[:], P, KEYS)
                take(mk_t[64:96, :, :], 32, KEYS, lambda b: ps[0:32, b * BANK:b * BANK + KEYS].unsqueeze(1).to_broadcast([32, 4, KEYS]))
                for t in range(T):
                    take(z_mq[:, t, :], P, 384)
                for h in range(4):
                    take(mk_t[0:64, h, :], 64, KEYS)
                for t in range(T + 1):
                    take(v_mla[:, t, :], P, BW)
                for h in range(4):
                    take(mq_t[0:96, h, :], 96, TOK)
                round_unit()
                attention(3)

                def load_branch(mp):
                    src = a["w_branch"][one, :, :, mp * 256:(mp + 1) * 256].rearrange("l b (k p) n -> p (l b k) n", p=P)
                    sc.dma_start(w_br[mp % 2][:], src).then_inc(branch_loaded[mp % 2].sem, 16)

                load_branch(0)
                for mp in range(4):
                    for n in range(NB):
                        for m in range(2):
                            i = 8 * mp + 2 * n + m
                            if i == 6:
                                take_o(3)
                                load_branch(1)
                            sc.wait_ge(gate_mm.sem, now(gate_mm, i + 1))
                            if i in (8, 16):
                                load_branch(i // 8 + 1)
                            if i >= 2:
                                sc.wait_ge(gate_read.sem, now(gate_read, i - 1))
                            act_(two(sig[:, i % 2, :]), tok2(4 * (i % 2)), ACT.Sigmoid, bias=vcol[:, BGATE + 8 * n + 2 * mp + m:BGATE + 8 * n + 2 * mp + m + 1])\
                                .then_inc(gate_sig.sem, 1)
                            if n == NB - 1 and m == 1:
                                for m_ in range(2):
                                    sc.wait_ge(mix_acc.sem, now(mix_acc, 2 * mp + m_ + 1))
                                    act_(mix_hi[:, 2 * mp + m_, :], acc[:, m_, :], ACT.Copy).then_inc(mix_h.sem, 1)
                        round_unit()
                for mp in range(3):
                    round_unit()
                norm(1)

                sc.wait_ge(pads_done.sem, now(pads_done, 1))
                for g, (j0, nj) in enumerate(UP_GROUPS):
                    for j in range(j0, j0 + nj):
                        sc.wait_ge(up_mm.sem, now(up_mm, j + 1))
                        if j >= 2:
                            sc.wait_ge(cv_done.sem, now(cv_done, j - 1))
                        s4 = 4 * (j % 2)
                        for part in range(2):
                            bias = vcol[:, BUP + FFT * part + j:BUP + FFT * part + j + 1]
                            u = u_pad[:, j % 2, part, :]
                            for d0, b, c0, n in ((1, 0, 0, CTX), (2 + CTX, 0, CTX, HALF - CTX), (2 + HALF, 1, 0, HALF)):
                                ins = act_(u[:, d0:d0 + n], bank(s4 + 2 * part + b, c0, c0 + n), ACT.Identity, bias=bias)
                        ins.then_inc(up_done.sem, 1)
                        round_unit()
                        sc.wait_ge(cv_done.sem, now(cv_done, j + 1))
                        if j:
                            sc.wait_ge(af_done.sem, now(af_done, j))
                        act_(usig[:], conv[:, 1, :], ACT.Sigmoid).then_inc(sg_done.sem, 1)
                        sc.wait_ge(af_done.sem, now(af_done, j + 1))
                        if j >= ACT_SLOTS:
                            before = next(g_ for g_, (a0, n_) in enumerate(UP_GROUPS) if a0 <= j - ACT_SLOTS < a0 + n_)
                            sc.wait_ge(down_mm.sem, now(down_mm, 8 * (before + 1)))
                        act_(a_hi[:, j % ACT_SLOTS, :], act[:], ACT.Copy).then_inc(ah_done.sem, 1)
                    for mp in range(4):
                        if nxt[0] < N_SPLIT:
                            round_unit()
                assert nxt[0] == N_SPLIT
                sc.wait_ge(cache_out.sem, now(cache_out, 16 * 10))
                sc.wait_ge(x_down.sem, now(x_down, 24))
            sc.wait_ge(yss_mm.sem, 1)
            act_(st5[:, 3, 0:T], bank(4, 0, T), ACT.Sqrt, bias=eps_c[:], scale=1.0 / D).then_inc(yst_done.sem, 1)
            sc.wait_ge(cache_out.sem, DEPTH * cache_out.per)

        @block.vector
        def _(ve):
            V = nc.vector
            tt, ts, stt = V.tensor_tensor, V.tensor_scalar, V.scalar_tensor_tensor
            V.memset(ones[:], 1.0).then_inc(made.sem, 1)
            V.memset(eps_c[:], EPS).then_inc(made.sem, 1)
            V.memset(lam_init[:], LAM0).then_inc(made.sem, 1)
            ve.wait_ge(made.sem, 3)
            ve.wait_ge(cond_t.sem, 1)
            V.tensor_copy(cond[:], bank(7, 0, 16)).then_inc(cond_raw.sem, 1)
            ve.wait_ge(cond_sig.sem, 1)
            ve.wait_ge(cond_raw.sem, 1)
            tt(cond[:], cond[:], stat[:, 0:2, :].rearrange("p a b -> p (a b)"), ALU.mult).then_inc(cond_done.sem, 1)
            ve.wait_ge(cond_done.sem, 1)
            cond_k = cond[:].rearrange("p (w k) -> p k w", w=2)
            V.tensor_copy(cond_r[:, :, 0:2], cond_k).then_inc(cond_done.sem, 1)
            ve.wait_ge(cond_done.sem, 2)
            tt(cond_r[:, :, 2:4], cond_k, cond_r[:, :, 0:2].bitcast(F32), ALU.subtract).then_inc(cond_done.sem, 1)
            base = ve.alloc_register("vector_base")
            ve.reg_mov(base, 0)
            for k in range(KD):
                ve.wait_ge(xin_done.sem, k + 1)
                if k >= 2:
                    ve.wait_ge(vstart.sem, 2 * k - 1)
                tt((sq if k else ss)[:], x[:, k, :], x[:, k, :], ALU.mult).then_inc(vstart.sem, 1)
                ve.wait_ge(vstart.sem, max(1, 2 * k))
                if k:
                    tt(ss[:], ss[:], sq[:], ALU.add).then_inc((vstart if k < KD - 1 else ss_done[0]).sem, 1)
            with ve.Fori(0, DEPTH) as li:
                now = counts(li)
                step = Steps(ve.snap(base))

                def take_mod(i):
                    ve.wait_ge(mod_t.sem, now(mod_t, i + 1))
                    c0 = mod_t_col(i)
                    tt(mod[:, 2 * i:2 * i + 2, :], ps[:, c0:c0 + 4].rearrange("p (m w) -> p m w", m=2),
                       vcol[:, BMOD + 2 * i:BMOD + 2 * i + 2].unsqueeze(2).to_broadcast([P, 2, 2]), ALU.add).then_inc(mod_done.sem, 1)

                def low_part(s):
                    ve.wait_ge(hi_done.sem, now(hi_done, s + 1))
                    n = unit_cols(SPLITS[s])
                    tt(w_lo[s % WS][:, 0:n], raw[SPLITS[s] % RAW][:, 0:n], w_hi[s % WS][:, 0:n].bitcast(F32), ALU.subtract)\
                        .then_inc(v_lo_done.sem, 1)

                def scale(i):
                    g0 = (GMIX, GFFN)[i]
                    stt(scl[:, i], mod[:, 24 * i + 8:24 * i + 16, :], 1.0, vcol[:, g0:g0 + 8].unsqueeze(2).to_broadcast([P, 8, 2]),
                        ALU.add, ALU.mult).then_inc(scl_done.sem, 1)

                def rstd(i):
                    ve.wait_ge(rms_done.sem, now(rms_done, i + 1))
                    V.reciprocal(st5[:, 1, 0:T], st5[:, 0, 0:T]).then_inc(vstep.sem, 1)
                    ve.wait_ge(vstep.sem, step())
                    tt(diag[:], ident.unsqueeze(1).to_broadcast([P, T, P]), st5[:, 1, 0:T].unsqueeze(2).to_broadcast([P, T, P]), ALU.mult)\
                        .then_inc(diag_done.sem, 1)

                def norm(i):
                    ve.wait_ge(bc_mm.sem, now(bc_mm, i + 1))
                    for k in range(KD + 1):
                        if k < KD:
                            if k >= 2:
                                ve.wait_ge(hf_done.sem, now(hf_done, 8 * i + k - 1))
                            tt(t1[:, k % 2, :], x[:, k, :], bank(6, 0, TOK), ALU.mult).then_inc(t1_done.sem, 1)
                        if k:
                            q = k - 1
                            ve.wait_ge(hh_done.sem, now(hh_done, 8 * i + q + 1))
                            tt(h_lo[:, q, :], hf[:, q % 2, :], h_hi[:, q, :].bitcast(F32), ALU.subtract).then_inc(h_done.sem, 1)

                def rope(zv, n, w, cos, sin, tmp, ready):
                    cosv = cos.rearrange("p (t c) -> p t c", t=NL)
                    sinv = sin.rearrange("p (t c) -> p t c", t=NL)
                    for t in range(NL):
                        ready(t + 1)
                        for i in range(4):
                            lo, other = i * w, (i ^ 1) * w
                            ins = tt(tmp[:, t, :, lo:lo + w], zv[:, t, :, other:other + w],
                                     sinv[:, t, lo:lo + w].unsqueeze(1).to_broadcast([P, n, w]), ALU.mult)
                        ins.then_inc(vstep.sem, 1)
                        ve.wait_ge(vstep.sem, step())
                        tt(zv[:, t], zv[:, t], cosv[:, t].unsqueeze(1).to_broadcast([P, n, 4 * w]), ALU.mult).then_inc(vstep.sem, 1)
                        ve.wait_ge(vstep.sem, step())
                        ins = tt(zv[:, t], zv[:, t], tmp[:, t], ALU.add)
                    return ins

                def attention(br):
                    head0 = 4 * T * (br - 1)

                    def softmax_bias(a_, m2):
                        _, t, h = HEADS[a_]
                        nk = P * len(key_blocks(br, t))
                        m = FIRST_MAP[a_] + m2
                        ve.wait_ge(s_mm.sem, now(s_mm, m + 1))
                        b = 2 * (m % 2)
                        if br == 1:
                            masked = [(j, mk) for j, (_, mk) in enumerate(window_blocks(t)) if mk]
                            for j, mk in masked:
                                ins = tt(bank(b, j * P, j * P + P), bank(b, j * P, j * P + P), c(mk), ALU.add)
                            if masked:
                                ins.then_inc(vstep.sem, 1)
                                ve.wait_ge(vstep.sem, step())
                        col = slice(m % 8, m % 8 + 1)
                        V.tensor_reduce(stat[:, 0, col], bank(b, 0, nk), AX.X, ALU.max).then_inc(vstep.sem, 1)
                        ve.wait_ge(vstep.sem, step())
                        if br == 1:
                            ts(stat[:, 0, col], stat[:, 0, col], SCALES[br], sink[:, h:h + 1], ALU.mult, ALU.max).then_inc(vstep.sem, 1)
                            ve.wait_ge(vstep.sem, step())
                            ts(stat[:, 1, col], stat[:, 0, col], -1.0, None, ALU.mult).then_inc(bias_done.sem, 1)
                        else:
                            ts(stat[:, 1, col], stat[:, 0, col], -SCALES[br], None, ALU.mult).then_inc(bias_done.sem, 1)

                    for i in range(STEPS):
                        if i >= 6 and (i - 3) % 4 == 3:
                            t = (i - 3) // 4
                            a_ = head0 + 4 * t
                            ve.wait_ge(pv_mm.sem, now(pv_mm, a_ + 4))
                            if t == 0:
                                ve.wait_ge(ot_mm.sem, now(ot_mm, 2 * br))
                            src = bank(6, 0, BW)
                            if br == 2:
                                den = dden[:, (a_ // 4) % 2, :]
                                ve.wait_ge(comb_done.sem, now(comb_done, 4 * t + 4))
                            else:
                                c0 = FIRST_MAP[a_] % 8
                                ve.wait_ge(exp_done.sem, now(exp_done, FIRST_MAP[a_] + 4))
                                den = stat[:, 2, c0:c0 + 4]
                                if br == 1:
                                    tt(stat[:, 4, c0:c0 + 4], den, stat[:, 3, c0:c0 + 4], ALU.add).then_inc(vstep.sem, 1)
                                    ve.wait_ge(vstep.sem, step())
                                    den = stat[:, 4, c0:c0 + 4]
                            V.reciprocal(orec[:], den).then_inc(vstep.sem, 1)
                            ve.wait_ge(vstep.sem, step())
                            tt(o_tm[:, t, :].rearrange("p (h d) -> p h d", h=4), src.rearrange("p (h d) -> p h d", h=4),
                               orec[:].unsqueeze(2).to_broadcast([P, 4, 64]), ALU.mult).then_inc(oev_done.sem, 1)
                        if br == 2 and 1 <= i <= 4 * T:
                            a_ = head0 + i - 1
                            nk = P * len(key_blocks(br, HEADS[a_][1]))
                            m = FIRST_MAP[a_]
                            ve.wait_ge(exp_done.sem, now(exp_done, m + 2))
                            c0, p0, p1 = m % 8, m % 4, (m + 1) % 4
                            V.reciprocal(stat[:, 4, c0:c0 + 1], stat[:, 2, c0 + 1:c0 + 2]).then_inc(vstep.sem, 1)
                            V.tensor_copy(dden[:, (a_ // 4) % 2, a_ % 4:a_ % 4 + 1], stat[:, 2, c0:c0 + 1])
                            ve.wait_ge(vstep.sem, step())
                            stt(stat[:, 5, c0:c0 + 1], stat[:, 4, c0:c0 + 1], lam[:], stat[:, 2, c0:c0 + 1], ALU.mult, ALU.mult).then_inc(vstep.sem, 1)
                            ve.wait_ge(vstep.sem, step())
                            stt(probs[:, p0, 0:nk], probs[:, p1, 0:nk], stat[:, 5, c0:c0 + 1], probs[:, p0, 0:nk], ALU.mult, ALU.add)\
                                .then_inc(comb_done.sem, 1)
                        if i < 4 * T:
                            for m2 in range(2 if br == 2 else 1):
                                softmax_bias(head0 + i, m2)
                        if i in MOD_STEPS[br]:
                            n_mod = 8 + 5 * (br - 1) + MOD_STEPS[br].index(i)
                            if n_mod > 8:
                                take_mod(n_mod - 1)

                heads = lambda ap: ap.rearrange("p t (h d) -> p (t h) d", h=4)
                wide20 = lambda ap: ap.unsqueeze(2).to_broadcast([P, 20, 64])

                ve.wait_ge(vec_t.sem, now(vec_t, 1))
                V.tensor_copy(vcol[:], bank(0, 0, 316)).then_inc(vec_done.sem, 1)
                ve.wait_ge(vec_done.sem, now(vec_done, 1))
                ve.wait_ge(small.sem, now(small, 16 * N_SMALL))
                for odd in range(2):
                    half_ = slice(64 * odd, 64 * odd + 64)
                    V.tensor_copy(decay[half_, 8:12], decay[half_, 0:8].rearrange("p (c e) -> p e c", e=2)[:, odd]).then_inc(vstep.sem, 1)
                    ve.wait_ge(vstep.sem, step())
                stt(dec_t[:, 0, :], decay[:], -1.0, decay[:], ALU.mult, ALU.max)
                dl = dlam[:].rearrange("p (a b) n -> p a b n", b=2)
                tt(dprod[:], dl[:, :, 0, :], dl[:, :, 1, :], ALU.mult).then_inc(vstep.sem, 1)
                ve.wait_ge(vstep.sem, step())
                V.tensor_reduce(dsum[:, 0:2], dprod[:], AX.X, ALU.add).then_inc(tab_arg.sem, 1)
                low_part(0)
                low_part(1)
                rstd(0)
                for i in range(8):
                    if i + 2 < 8:
                        low_part(i + 2)
                    take_mod(i)
                ve.wait_ge(mod_done.sem, now(mod_done, 8))
                scale(0)
                norm(0)
                ve.wait_ge(tab_exp.sem, now(tab_exp, 1))
                zc, s_, s2, q_ = (dec_t[:, i_, :] for i_ in (1, 2, 3, 0))
                ts(s2, zc, 2.0, None, ALU.add).then_inc(vstep.sem, 1)
                ve.wait_ge(vstep.sem, step())
                V.reciprocal(q_, s2).then_inc(vstep.sem, 1)
                ve.wait_ge(vstep.sem, step())
                tt(s_, zc, q_, ALU.mult).then_inc(vstep.sem, 1)
                ve.wait_ge(vstep.sem, step())
                tt(s2, s_, s_, ALU.mult).then_inc(vstep.sem, 1)
                ve.wait_ge(vstep.sem, step())
                ts(q_, s2, 1.0 / 19, None, ALU.mult).then_inc(vstep.sem, 1)
                ve.wait_ge(vstep.sem, step())
                for n in (17, 15, 13, 11, 9, 7, 5, 3):
                    stt(q_, q_, 1.0 / n, s2, ALU.add, ALU.mult).then_inc(vstep.sem, 1)
                    ve.wait_ge(vstep.sem, step())
                stt(q_, q_, 1.0, s_, ALU.add, ALU.mult).then_inc(vstep.sem, 1)
                ve.wait_ge(vstep.sem, step())
                ts(s_, decay[:], 0.0, None, ALU.min).then_inc(vstep.sem, 1)
                ve.wait_ge(vstep.sem, step())
                stt(lgam[:], q_, -2.0, s_, ALU.mult, ALU.add).then_inc(tab_arg.sem, 1)
                stt(lam[:], dsum[:, 2:3], -1.0, dsum[:, 3:4], ALU.mult, ALU.add).then_inc(vstep.sem, 1)
                ve.wait_ge(vstep.sem, step())
                tt(lam[:], lam[:], lam_init[:], ALU.subtract).then_inc(vstep.sem, 1)
                ve.wait_ge(vstep.sem, step())
                ts(one_minus[:], lam_init[:], -1.0, 1.0, ALU.mult, ALU.add).then_inc(vstep.sem, 1)
                ve.wait_ge(vstep.sem, step())
                ts(gd[:], g_diff[:], one_minus[:], None, ALU.mult).then_inc(vstep.sem, 1)
                ve.wait_ge(vstep.sem, step())

                ve.wait_ge(tab_exp.sem, now(tab_exp, 2))
                K8 = 64 ** -0.5
                stt(decay_f[:], decay_f[:], K8, c("upf").unsqueeze(1).to_broadcast([P, 4, P]), ALU.mult, ALU.mult)
                stt(decay_b[:], decay_b[:], K8, c("upb").unsqueeze(1).to_broadcast([P, 4, P]), ALU.mult, ALU.mult).then_inc(vstep.sem, 1)
                ve.wait_ge(vstep.sem, step())
                tt(dmask[:], decay_f[:], decay_b[:], ALU.add).then_inc(vstep.sem, 1)
                ve.wait_ge(vstep.sem, step())
                ts(kdec[:], kdec[:], K8, None, ALU.mult).then_inc(vstep.sem, 1)
                ve.wait_ge(vstep.sem, step())
                for t in range(T):
                    ve.wait_ge(z_done.sem, now(z_done, t + 1))
                    if t >= 2:
                        ve.wait_ge(u_mm.sem, now(u_mm, t - 1))
                    tt(kd[:, t % 2].rearrange("p (r h) d -> p r h d", r=2),
                       z[0][:, t, 256:512].rearrange("p (h d) -> p h d", h=4).unsqueeze(1).to_broadcast([P, 2, 4, 64]),
                       kdec[:].unsqueeze(3).to_broadcast([P, 2, 4, 64]), ALU.mult).then_inc(kd_done.sem, 1)
                u_at = lambda t, r: bank(4 + t // 2, 256 * (t % 2) + 128 * r, 256 * (t % 2) + 128 * r + 128).rearrange("p (j d) -> p j d", j=2)
                ve.wait_ge(u_mm.sem, now(u_mm, T))
                V.tensor_copy(state_c[:].rearrange("p c d -> p (c d)"), bank(4, 0, 256)).then_inc(st_out.sem, 1)
                for r in range(2):
                    for n in (range(1, NL) if r == 0 else range(NL - 2, -1, -1)):
                        before, t = (n - 1, n) if r == 0 else (n + 1, n + 2)
                        for j in range(2):
                            ins = stt(states[:, r, n, j, :], state_of(r, before)[:, j, :], cdec[:, 2 * r + j:2 * r + j + 1],
                                      u_at(t, r)[:, j, :], ALU.mult, ALU.add)
                        if r == 1 and n == 0:
                            ins.then_inc(s_done.sem, 1)
                        else:
                            ins.then_inc(vstep.sem, 1)
                            ve.wait_ge(vstep.sem, step())
                for t in range(T):
                    ve.wait_ge(rs_mm.sem, now(rs_mm, t + 1))
                    if t >= 2:
                        ve.wait_ge(ro_mm.sem, now(ro_mm, t - 1))
                    src = ps[:, 2 * (t % 2) * BANK:(2 * (t % 2) + 2) * BANK].rearrange("p (e n) -> p e n", e=2)[:, :, 0:256]
                    tt(st_dec[:, t % 2].rearrange("p (e j) n -> p e (j n)", e=2), src, dmask[:].rearrange("p (e j) n -> p e (j n)", e=2), ALU.mult)\
                        .then_inc(rst_done.sem, 1)
                    ve.wait_ge(rt_done.sem, now(rt_done, t + 1))
                    tt(q_dec[:, t % 2].rearrange("p (r j) n -> p r j n", r=2), rqk[:, 0:2, t * P:(t + 1) * P].unsqueeze(1).to_broadcast([P, 2, 2, P]),
                       qdec[:].rearrange("p (r j) n -> p r j n", r=2), ALU.mult).then_inc(rst_done.sem, 1)

                ve.wait_ge(ro_done.sem, now(ro_done, T))
                V.tensor_reduce(st5[:, 0, :], heads(o_tm[:]), AX.X, ALU.add).then_inc(vstep.sem, 1)
                ve.wait_ge(vstep.sem, step())
                ts(st5[:, 1, :], st5[:, 0, :], 1.0 / 64, None, ALU.mult).then_inc(vstep.sem, 1)
                ve.wait_ge(vstep.sem, step())
                tt(heads(post[:]), heads(o_tm[:]), wide20(st5[:, 1, :]), ALU.subtract).then_inc(post_in.sem, 1)
                ve.wait_ge(post_act.sem, now(post_act, 1))
                V.tensor_reduce(st5[:, 2, :], heads(o_tm[:]), AX.X, ALU.add).then_inc(post_in.sem, 1)
                ve.wait_ge(post_act.sem, now(post_act, 2))
                V.reciprocal(st5[:, 0, :], st5[:, 3, :]).then_inc(vstep.sem, 1)
                ve.wait_ge(vstep.sem, step())
                tt(heads(post[:]), heads(post[:]), wide20(st5[:, 0, :]), ALU.mult).then_inc(vstep.sem, 1)
                ve.wait_ge(vstep.sem, step())
                tt(post[:], post[:], z[1][:, :, 256:512], ALU.mult).then_inc(vstep.sem, 1)
                ve.wait_ge(vstep.sem, step())
                ve.wait_ge(post_act.sem, now(post_act, 3))
                tt(o_tm[:], post[:], o_tm[:], ALU.mult).then_inc(ret_o.sem, 1)

                ve.wait_ge(ret_o.sem, now(ret_o, 1))
                rope(z[0][:, 1:T, 0:384].rearrange("p t (n c) -> p t n c", c=64), 6, 16, c("c16"), c("s16"),
                     rope_tmp[1][:].rearrange("p t (n c) -> p t n c", c=64),
                     lambda t: ve.wait_ge(z_done.sem, now(z_done, 2 * T + t + 1))).then_inc(rope_done.sem, 1)
                attention(1)

                rope(z[0][:, 1:T, :].rearrange("p t (n c) -> p t n c", c=32), 16, 8, c("c8"), c("s8"),
                     rope_tmp[2][:].rearrange("p t (n c) -> p t n c", c=32),
                     lambda t: ve.wait_ge(z_done.sem, now(z_done, 3 * T + t + 1))).then_inc(rope_done.sem, 1)
                attention(2)
                ve.wait_ge(oev_done.sem, now(oev_done, 2 * T))
                V.tensor_copy(stat[:, 6, 0:1], stat[:, 4, 0:1]).then_inc(post_in.sem, 1)
                ve.wait_ge(post_act.sem, now(post_act, 4))
                V.tensor_reduce(st5[:, 2, :], heads(post[:]), AX.X, ALU.add).then_inc(post_in.sem, 1)
                ve.wait_ge(post_act.sem, now(post_act, 5))
                V.reciprocal(st5[:, 0, :], st5[:, 3, :]).then_inc(vstep.sem, 1)
                ve.wait_ge(vstep.sem, step())
                tt(heads(o_tm[:]), heads(o_tm[:]), wide20(st5[:, 0, :]), ALU.mult).then_inc(vstep.sem, 1)
                ve.wait_ge(vstep.sem, step())
                tt(heads(o_tm[:]), heads(o_tm[:]), gd[:].unsqueeze(1).to_broadcast([P, 20, 64]), ALU.mult).then_inc(diff_o.sem, 1)

                ve.wait_ge(prep_act.sem, now(prep_act, 1))
                V.tensor_reduce(st5[:, 0, 0:T], post[:], AX.X, ALU.add).then_inc(prep_in.sem, 1)
                ve.wait_ge(prep_act.sem, now(prep_act, 2))
                V.reciprocal(st5[:, 0, 0:T], st5[:, 1, 0:T]).then_inc(vstep.sem, 1)
                ve.wait_ge(vstep.sem, step())
                zq, zk = z[1][:, :, 256:512], z5[:, :, 0:128]
                tt(zq, zq, st5[:, 0, 0:T].unsqueeze(2).to_broadcast([P, T, BW]), ALU.mult).then_inc(vstep.sem, 1)
                ve.wait_ge(vstep.sem, step())
                tt(zq, zq, g_mq[:].unsqueeze(1).to_broadcast([P, T, BW]), ALU.mult)
                ve.wait_ge(prep_act.sem, now(prep_act, 3))
                V.tensor_reduce(st5[:, 0, T:2 * T], sq_kv[:], AX.X, ALU.add).then_inc(prep_in.sem, 1)
                ve.wait_ge(z_done.sem, now(z_done, 6 * T))
                rope(z5[:, 1:T, 128:160].unsqueeze(2), 1, 8, c("c8"), c("s8"), rope_tmp[4][:], lambda t: None)
                ve.wait_ge(prep_act.sem, now(prep_act, 4))
                V.reciprocal(st5[:, 0, T:2 * T], st5[:, 1, T:2 * T]).then_inc(vstep.sem, 1)
                ve.wait_ge(vstep.sem, step())
                tt(zk, zk, st5[:, 0, T:2 * T].unsqueeze(2).to_broadcast([P, T, P]), ALU.mult).then_inc(vstep.sem, 1)
                ve.wait_ge(vstep.sem, step())
                tt(zk, zk, g_mkv[:].unsqueeze(1).to_broadcast([P, T, P]), ALU.mult).then_inc(prep_done.sem, 1)
                rope(z_mq[:, 1:T, :].rearrange("p t (h c) -> p t h c", h=4)[:, :, :, 64:96], 4, 8, c("c8"), c("s8"), rope_tmp[3][:],
                     lambda t: ve.wait_ge(mla_done.sem, now(mla_done, 4 + t + 1)))\
                    .then_inc(rope_done.sem, 1)
                attention(3)
                take_mod(23)
                ve.wait_ge(mod_done.sem, now(mod_done, 24))
                scale(1)
                ve.wait_ge(oev_done.sem, now(oev_done, 3 * T))

                for mp in range(4):
                    for n in range(NB):
                        for m in range(2):
                            i = 8 * mp + 2 * n + m
                            ve.wait_ge(gate_sig.sem, now(gate_sig, i + 1))
                            dst = acc[:, m, :] if n == 0 else gprod[:]
                            if n == 0 and mp:
                                ve.wait_ge(mix_done.sem, now(mix_done, 2 * mp - 1 + m))
                            tt(two(dst), two(sig[:, i % 2, :]), tok2(4 * (i % 2) + 2), ALU.mult).then_inc(gate_read.sem, 1)
                            if n:
                                ve.wait_ge(gate_read.sem, now(gate_read, i + 1))
                                ins = tt(acc[:, m, :], acc[:, m, :], gprod[:], ALU.add)
                                if n == NB - 1:
                                    ins.then_inc(mix_acc.sem, 1)
                                    ve.wait_ge(mix_acc.sem, now(mix_acc, 2 * mp + m + 1))
                                else:
                                    ins.then_inc(vstep.sem, 1)
                                    ve.wait_ge(vstep.sem, step())
                    for m in range(2):
                        ve.wait_ge(mix_h.sem, now(mix_h, 2 * mp + m + 1))
                        tt(mix_lo[:, 2 * mp + m, :], acc[:, m, :], mix_hi[:, 2 * mp + m, :].bitcast(F32), ALU.subtract)\
                            .then_inc(mix_done.sem, 1)

                def add_square(m):
                    tt((sq if m else ss)[:], x[:, m, :], x[:, m, :], ALU.mult).then_inc(vstep.sem, 1)
                    ve.wait_ge(vstep.sem, step())
                    return tt(ss[:], ss[:], sq[:], ALU.add) if m else None

                def add_to_x(k, gate0, pieces):
                    for w, c0, src in pieces:
                        n = src.shape[1]
                        ins = stt(x[:, k, c0:c0 + n], src, mod[:, gate0 + k, w:w + 1], x[:, k, c0:c0 + n], ALU.mult, ALU.add)
                    return ins

                for m in range(KD):
                    ve.wait_ge(out_mm.sem, now(out_mm, m + 1))
                    b = 2 * (m % 2)
                    add_to_x(m, 16, ((0, 0, bank(b, 0, CTX)), (1, CTX, bank(b, CTX, HALF)), (1, HALF, bank(b + 1, 0, HALF))))\
                        .then_inc(x_out.sem, 1)
                    ve.wait_ge(x_out.sem, now(x_out, m + 1))
                    ins = add_square(m)
                    if m == KD - 1:
                        ins.then_inc(ss_done[1].sem, 1)
                    elif m:
                        ins.then_inc(vstep.sem, 1)
                        ve.wait_ge(vstep.sem, step())
                rstd(1)
                norm(1)
                ve.wait_ge(h_done.sem, now(h_done, 16))
                for col, n in ((0, 1), (1 + CTX, 1), (UB - 2, 2)):
                    ins = V.memset(u_pad[:, :, :, col:col + n], 0.0)
                ins.then_inc(pads_done.sem, 1)

                for g, (j0, nj) in enumerate(UP_GROUPS):
                    for j in range(j0, j0 + nj):
                        ve.wait_ge(up_done.sem, now(up_done, j + 1))
                        for part in range(2):
                            col = lambda b0: vcol[:, b0 + FFT * part + j:b0 + FFT * part + j + 1]
                            u, cv = u_pad[:, j % 2, part, :], conv[:, part, :]
                            ts(cv, u[:, 0:PADDED], col(WCONV[0]), col(BCONV), ALU.mult, ALU.add).then_inc(vstep.sem, 1)
                            ve.wait_ge(vstep.sem, step())
                            stt(cv, u[:, 1:1 + PADDED], col(WCONV[1]), cv, ALU.mult, ALU.add).then_inc(vstep.sem, 1)
                            ve.wait_ge(vstep.sem, step())
                            ins = stt(cv, u[:, 2:2 + PADDED], col(WCONV[2]), cv, ALU.mult, ALU.add)
                            if part == 0:
                                ins.then_inc(vstep.sem, 1)
                                ve.wait_ge(vstep.sem, step())
                        ins.then_inc(cv_done.sem, 1)
                        ve.wait_ge(cv_done.sem, now(cv_done, j + 1))
                        ve.wait_ge(sg_done.sem, now(sg_done, j + 1))
                        tt(act[:], conv[:, 1, :], usig[:], ALU.mult).then_inc(vstep.sem, 1)
                        ve.wait_ge(vstep.sem, step())
                        tt(act[:], act[:], conv[:, 0, :], ALU.mult).then_inc(af_done.sem, 1)
                        ve.wait_ge(ah_done.sem, now(ah_done, j + 1))
                        tt(a_lo[:, j % ACT_SLOTS, :], act[:], a_hi[:, j % ACT_SLOTS, :].bitcast(F32), ALU.subtract).then_inc(al_done.sem, 1)
                    for m in range(8):
                        ve.wait_ge(down_mm.sem, now(down_mm, 8 * g + m + 1))
                        b = 2 * (m % 2)
                        add_to_x(m, 40, ((0, 0, bank(b, 0, CTX)), (1, CTX, bank(b, CTX + 1, HALF + 2)), (1, HALF + 1, bank(b + 1, 0, HALF - 1))))\
                            .then_inc(x_down.sem, 1)
                        if g == len(UP_GROUPS) - 1:
                            ve.wait_ge(x_down.sem, now(x_down, 8 * g + m + 1))
                            ins = add_square(m)
                            if m == KD - 1:
                                ins.then_inc(ss_done[0].sem, 1)
                            elif m:
                                ins.then_inc(vstep.sem, 1)
                                ve.wait_ge(vstep.sem, step())
                ts(lam_init[:], lam_init[:], LAM_DECAY, 0.8 * (1 - LAM_DECAY), ALU.mult, ALU.add).then_inc(vstep.sem, 1)
                ve.wait_ge(vstep.sem, step())
                ve.reg_add(base, base, step.n)
            ve.wait_ge(gfin.sem, 16)
            ve.wait_ge(yst_done.sem, 1)
            V.reciprocal(st5[:, 1, 0:T], st5[:, 3, 0:T]).then_inc(yrec.sem, 1)
            ve.wait_ge(yrec.sem, 1)
            for t in range(T):
                ve.wait_ge(yt_mm.sem, t + 1)
                stt(y_tm[:, t, :], bank(2 * (t % 4), 0, 2 * BANK), st5[:, 1, t:t + 1], g_fin[:], ALU.mult, ALU.mult).then_inc(y_done.sem, 1)


_INS = ["x_prompt", "x_sample", "state_ret", "cache_win_k", "cache_win_v", "cache_diff_k", "cache_diff_v", "cache_mla_ckv",
        "cache_mla_krope", "c", "c_ctx", "w_mod", "b_mod", "g_mix", "w_in", "ret_decay", "win_sink", "diff_lambda", "g_diff",
        "g_mla_q", "w_mla_uq", "g_mla_kv", "w_mla_ukv", "w_branch", "w_gate", "b_gate", "w_out", "g_ffn", "w_up", "b_up",
        "w_conv", "b_conv", "w_down", "g_final"]
_OUTS = [(1, CTX, D), (1, LAT, D), (1, DEPTH, 2, 4, 64, 64), (1, DEPTH, CTX, 2, 64), (1, DEPTH, CTX, 2, 64),
         (1, DEPTH, CTX, 4, 64), (1, DEPTH, CTX, 4, 64), (1, DEPTH, CTX, 128), (1, DEPTH, CTX, 32)]


def kernel(**inputs):
    import concourse.bacc as bacc
    from concourse.bass_utils import run_bass_kernel_spmd

    nc = bacc.Bacc("TRN2", target_bir_lowering=False, num_devices=1, dynamic_dma_scratch_size=1024)
    arrays = {name: np.ascontiguousarray(inputs[name]) for name in _INS}
    arrays["const"] = shape_constants()
    aps = {name: nc.dram_tensor(f"in_{name}", v.shape, F32, kind="ExternalInput").ap() for name, v in arrays.items()}
    outs = [nc.dram_tensor(f"out_{i}", shape, F32, kind="ExternalOutput").ap() for i, shape in enumerate(_OUTS)]
    build(nc, aps, outs)
    r = run_bass_kernel_spmd(nc, [{f"in_{name}": v for name, v in arrays.items()}], core_ids=[0])
    return tuple(r.results[0][f"out_{i}"] for i in range(len(_OUTS)))
```
